# Optimizing a Trainium2 kernel written in Bass

```python
import jax, jax.numpy as jnp
from jax import lax
import numpy as np
import math

D_MODEL = 2048
BATCH = 1
SEQ = 256
DEPTH = 1

CHUNK = 64
Q_BLOCK = 128
D_MIX = D_MODEL
HGRN_WIDTH = D_MIX // 2
HGRN_DK = 128
HGRN_HEADS = HGRN_WIDTH // HGRN_DK
HGRN_DV = HGRN_WIDTH // HGRN_HEADS
FOX_WIDTH = D_MIX - HGRN_WIDTH
FOX_HEAD_DIM = 128
FOX_HEADS = FOX_WIDTH // FOX_HEAD_DIM
D_FF = ((8 * D_MODEL // 3 + 255) // 256) * 256
CONV_WIDTH = 3
EPS = 1e-6
FOX_GATE_BIAS_OFFSET = 2.0
IN_SIZES = (HGRN_HEADS * HGRN_DK, HGRN_HEADS * HGRN_DK, HGRN_WIDTH, HGRN_WIDTH,
            FOX_WIDTH, FOX_WIDTH, FOX_WIDTH, FOX_HEADS)
D_IN = sum(IN_SIZES)


def rmsnorm(x, gain):
    x32 = x.astype(jnp.float32)
    y = x32 * lax.rsqrt(jnp.mean(x32 * x32, axis=-1, keepdims=True) + EPS) * gain.astype(jnp.float32)
    return y.astype(x.dtype)

def gla_chunkwise(q, k, v, logf):
    B, H, L, DK = q.shape
    DV = v.shape[-1]
    N = L // CHUNK
    r = lambda t: t.reshape(B, H, N, CHUNK, t.shape[-1])
    q, k, v, logf = r(q), r(k), r(v), r(logf)
    b = jnp.cumsum(logf, axis=-2)
    b_last = b[..., -1:, :]
    q_dec = q * jnp.exp(b)
    k_dec = k * jnp.exp(-b)
    k_end = k * jnp.exp(b_last - b)
    mask = jnp.tril(jnp.ones((CHUNK, CHUNK), dtype=bool))
    attn = jnp.einsum('bhnck,bhnsk->bhncs', q_dec, k_dec)
    attn = jnp.where(mask, attn, 0.0)
    o_intra = jnp.einsum('bhncs,bhnsv->bhncv', attn, v)
    chunk_decay = jnp.exp(b_last[..., 0, :])

    def step(S, xs):
        qd, ke, vv, dc = xs
        o = jnp.einsum('bhck,bhkv->bhcv', qd, S)
        S = dc[..., None] * S + jnp.einsum('bhck,bhcv->bhkv', ke, vv)
        return S, o

    xs = (jnp.moveaxis(q_dec, 2, 0), jnp.moveaxis(k_end, 2, 0),
          jnp.moveaxis(v, 2, 0), jnp.moveaxis(chunk_decay, 2, 0))
    S0 = jnp.zeros((B, H, DK, DV), jnp.float32)
    _, o_inter = lax.scan(step, S0, xs)
    o = o_intra + jnp.moveaxis(o_inter, 0, 2)
    return o.reshape(B, H, L, DV)

def hgrn2_mixer(q, f_logit, inp, g, lb, norm_gain):
    B, L, _ = q.shape
    dt = q.dtype
    heads = lambda t, d: t.reshape(B, L, HGRN_HEADS, d).transpose(0, 2, 1, 3).astype(jnp.float32)
    qh = heads(q, HGRN_DK) * (HGRN_DK ** -0.5)
    zh = heads(f_logit, HGRN_DK)
    vh = heads(inp, HGRN_DV)
    lbh = lb.astype(jnp.float32).reshape(HGRN_HEADS, HGRN_DK)[None, :, None, :]
    f = lbh + (1.0 - lbh) * jax.nn.sigmoid(zh)
    kh = 1.0 - f
    o = gla_chunkwise(qh, kh, vh, jnp.log(f))
    o = o * lax.rsqrt(jnp.mean(o * o, axis=-1, keepdims=True) + EPS) * norm_gain.astype(jnp.float32)
    o = o * jax.nn.silu(heads(g, HGRN_DV))
    return o.transpose(0, 2, 1, 3).reshape(B, L, HGRN_WIDTH).astype(dt)

def fox_mixer(q, k, v, f_logit, gate_bias):
    B, L, _ = q.shape
    dt = q.dtype
    heads = lambda t: t.reshape(B, L, FOX_HEADS, FOX_HEAD_DIM).transpose(0, 2, 1, 3)
    qh, kh, vh = heads(q), heads(k), heads(v)
    logf = jax.nn.log_sigmoid(f_logit.astype(jnp.float32) + gate_bias.astype(jnp.float32))
    c = jnp.cumsum(logf, axis=1).transpose(0, 2, 1)
    scale = FOX_HEAD_DIM ** -0.5
    kpos = jnp.arange(L)

    def one_block(blk):
        start = blk * Q_BLOCK
        qb = lax.dynamic_slice_in_dim(qh, start, Q_BLOCK, axis=2)
        cb = lax.dynamic_slice_in_dim(c, start, Q_BLOCK, axis=2)
        s = jnp.einsum('bhqd,bhkd->bhqk', qb, kh).astype(jnp.float32) * scale
        s = s + cb[..., :, None] - c[..., None, :]
        qpos = start + jnp.arange(Q_BLOCK)
        s = jnp.where(kpos[None, :] <= qpos[:, None], s, -jnp.inf)
        p = jax.nn.softmax(s, axis=-1)
        return jnp.einsum('bhqk,bhkd->bhqd', p.astype(vh.dtype), vh)

    out = lax.map(one_block, jnp.arange(L // Q_BLOCK))
    out = out.transpose(1, 0, 3, 2, 4).reshape(B, L, FOX_WIDTH)
    return out.astype(dt)

def conv_ffn(h, w_gate, w_up, conv_w, conv_b, w_down):
    L = h.shape[1]
    a = h @ w_gate
    a_pad = jnp.pad(a, ((0, 0), (CONV_WIDTH - 1, 0), (0, 0)))
    a = sum(conv_w[j] * a_pad[:, j:j + L] for j in range(CONV_WIDTH)) + conv_b
    return (jax.nn.silu(a) * (h @ w_up)) @ w_down

def first_inputs(seed: int = 0) -> dict:
    key = jax.random.key(seed)
    ks = jax.random.split(key, 16)
    nrm = lambda k, shape, s: jax.random.normal(k, shape, jnp.float32) * s
    return {
        'x': nrm(ks[0], (BATCH, SEQ, D_MODEL), 1.0),
        'norm1_gain': 1.0 + nrm(ks[1], (DEPTH, D_MODEL), 0.02),
        'w_in': nrm(ks[2], (DEPTH, D_MODEL, D_IN), D_MODEL ** -0.5),
        'hgrn_lb_param': nrm(ks[3], (DEPTH + 1, HGRN_HEADS * HGRN_DK), 0.5),
        'hgrn_norm_gain': 1.0 + nrm(ks[4], (DEPTH, HGRN_DV), 0.02),
        'fox_gate_bias': FOX_GATE_BIAS_OFFSET + nrm(ks[5], (DEPTH, FOX_HEADS), 0.1),
        'w_out': nrm(ks[6], (DEPTH, D_MIX, D_MODEL), D_MIX ** -0.5),
        'norm2_gain': 1.0 + nrm(ks[7], (DEPTH, D_MODEL), 0.02),
        'w_ffn_gate': nrm(ks[8], (DEPTH, D_MODEL, D_FF), D_MODEL ** -0.5),
        'w_ffn_up': nrm(ks[9], (DEPTH, D_MODEL, D_FF), D_MODEL ** -0.5),
        'ffn_conv_w': nrm(ks[10], (DEPTH, CONV_WIDTH, D_FF), CONV_WIDTH ** -0.5),
        'ffn_conv_b': nrm(ks[11], (DEPTH, D_FF), 0.02),
        'w_ffn_down': nrm(ks[12], (DEPTH, D_FF, D_MODEL), D_FF ** -0.5),
        'final_norm_gain': 1.0 + nrm(ks[13], (D_MODEL,), 0.02),
    }

def first_block(x, norm1_gain, w_in, hgrn_lb_param, hgrn_norm_gain, fox_gate_bias, w_out,
              norm2_gain, w_ffn_gate, w_ffn_up, ffn_conv_w, ffn_conv_b, w_ffn_down,
              final_norm_gain):
    split_points = [int(v) for v in np.cumsum(IN_SIZES)[:-1]]
    lb_all = jnp.cumsum(jax.nn.softmax(hgrn_lb_param.astype(jnp.float32), axis=0), axis=0)
    for l in range(DEPTH):
        h = rmsnorm(x, norm1_gain[l])
        proj = h @ w_in[l]
        q_a, f_a, i_a, g_a, q_b, k_b, v_b, f_b = jnp.split(proj, split_points, axis=-1)
        o_a = hgrn2_mixer(q_a, f_a, i_a, g_a, lb_all[l], hgrn_norm_gain[l])
        o_b = fox_mixer(q_b, k_b, v_b, f_b, fox_gate_bias[l])
        x = x + jnp.concatenate([o_a, o_b], axis=-1) @ w_out[l]
        h = rmsnorm(x, norm2_gain[l])
        x = x + conv_ffn(h, w_ffn_gate[l], w_ffn_up[l], ffn_conv_w[l], ffn_conv_b[l], w_ffn_down[l])
    return rmsnorm(x, final_norm_gain)


DEPTH_2 = 2

N_MEM = 256
N_A_LAYERS = DEPTH_2 // 2
N_B_LAYERS = DEPTH_2 - N_A_LAYERS
HEAD_DIM = 128
MIX_WIDTH = D_MODEL
MEM_HEADS = 4
MEM_WIDTH = MEM_HEADS * HEAD_DIM
BRANCH_WIDTH = MIX_WIDTH - MEM_WIDTH
POOL_WINDOWS = (2, 4, 8, 16)
N_POOL_GROUPS = len(POOL_WINDOWS)
POOL_GROUP = BRANCH_WIDTH // N_POOL_GROUPS
MOBA_HEADS = BRANCH_WIDTH // HEAD_DIM
MOBA_BLOCK = 256
MOBA_TOPK = 3
Q_CHUNK = 64
IN_WIDTH = 2 * BRANCH_WIDTH + 2 * MEM_WIDTH
DEEPNORM_ALPHA = (2 * DEPTH_2) ** 0.25
DEEPNORM_BETA = (8 * DEPTH_2) ** -0.25
LN_EPS = 1e-5


def layer_norm(x, g, b):
    xf = x.astype(jnp.float32)
    mu = xf.mean(-1, keepdims=True)
    var = jnp.square(xf - mu).mean(-1, keepdims=True)
    return ((xf - mu) * lax.rsqrt(var + LN_EPS) * g + b).astype(x.dtype)

def multiscale_pool(u, pool_w, pool_scale):
    B, S, _ = u.shape
    uf = u.astype(jnp.float32)
    cs = jnp.concatenate([jnp.zeros((B, 1, BRANCH_WIDTH), jnp.float32),
                          jnp.cumsum(uf, axis=1)], axis=1)
    t = jnp.arange(S)
    outs = []
    for g, w in enumerate(POOL_WINDOWS):
        sl = slice(g * POOL_GROUP, (g + 1) * POOL_GROUP)
        csg = cs[:, :, sl]
        lo = jnp.maximum(t + 1 - w, 0)
        cnt = (t + 1 - lo).astype(jnp.float32)
        outs.append((csg[:, 1:] - csg[:, lo]) / cnt[None, :, None] - uf[:, :, sl])
    pooled = jnp.stack(outs, axis=2).astype(u.dtype)
    mixed = jnp.einsum('bsgc,gcd->bsgd', pooled, pool_w).reshape(B, S, BRANCH_WIDTH)
    return mixed * pool_scale

def memory_attention(mq, mem, w_mem_kv):
    B, S, _ = mq.shape
    M = mem.shape[1]
    mk, mv = jnp.split(mem @ w_mem_kv, 2, axis=-1)
    q = mq.reshape(B, S, MEM_HEADS, HEAD_DIM)
    k = mk.reshape(B, M, MEM_HEADS, HEAD_DIM)
    v = mv.reshape(B, M, MEM_HEADS, HEAD_DIM)
    s = jnp.einsum('bshd,bmhd->bhsm', q, k).astype(jnp.float32) * (HEAD_DIM ** -0.5)
    p = jax.nn.softmax(s, axis=-1).astype(v.dtype)
    return jnp.einsum('bhsm,bmhd->bshd', p, v).reshape(B, S, MEM_WIDTH)

def moba_shared_kv(h, w_kv):
    B, S, _ = h.shape
    k, v = jnp.split(h @ w_kv, 2, axis=-1)
    nb = -(-S // MOBA_BLOCK)
    pad = nb * MOBA_BLOCK - S
    k = k.reshape(B, S, MOBA_HEADS, HEAD_DIM).transpose(0, 2, 1, 3)
    v = v.reshape(B, S, MOBA_HEADS, HEAD_DIM).transpose(0, 2, 1, 3)
    k = jnp.pad(k, ((0, 0), (0, 0), (0, pad), (0, 0)))
    v = jnp.pad(v, ((0, 0), (0, 0), (0, pad), (0, 0)))
    k_blocks = k.reshape(B, MOBA_HEADS, nb, MOBA_BLOCK, HEAD_DIM)
    v_blocks = v.reshape(B, MOBA_HEADS, nb, MOBA_BLOCK, HEAD_DIM)
    k_mean = k_blocks.astype(jnp.float32).mean(axis=3).astype(k.dtype)
    return k_blocks, v_blocks, k_mean

def moba_attention(q_in, k_blocks, v_blocks, k_mean):
    B, S, _ = q_in.shape
    H = MOBA_HEADS
    nb = k_blocks.shape[2]
    n_sel = min(MOBA_TOPK, nb)
    scale = HEAD_DIM ** -0.5
    q = q_in.reshape(B, S, H, HEAD_DIM).transpose(0, 2, 1, 3)
    b_idx = jnp.arange(B)[:, None, None, None]
    h_idx = jnp.arange(H)[None, :, None, None]
    blk_ids = jnp.arange(nb)
    blk_offs = jnp.arange(MOBA_BLOCK)

    def chunk(c):
        start = c * Q_CHUNK
        qc = lax.dynamic_slice_in_dim(q, start, Q_CHUNK, axis=2)
        own = start // MOBA_BLOCK
        q_pos = start + jnp.arange(Q_CHUNK)
        gate = jnp.einsum('bhqd,bhnd->bhqn', qc, k_mean).astype(jnp.float32)
        gate = jnp.where(blk_ids < own, gate, -jnp.inf)
        _, sel = lax.top_k(gate, n_sel)
        valid = sel < own
        kg = k_blocks[b_idx, h_idx, sel]
        vg = v_blocks[b_idx, h_idx, sel]
        s_sel = jnp.einsum('bhqd,bhqjkd->bhqjk', qc, kg).astype(jnp.float32) * scale
        s_sel = jnp.where(valid[..., None], s_sel, -jnp.inf)
        s_sel = s_sel.reshape(B, H, Q_CHUNK, n_sel * MOBA_BLOCK)
        k_own = lax.dynamic_index_in_dim(k_blocks, own, axis=2, keepdims=False)
        v_own = lax.dynamic_index_in_dim(v_blocks, own, axis=2, keepdims=False)
        s_own = jnp.einsum('bhqd,bhkd->bhqk', qc, k_own).astype(jnp.float32) * scale
        k_pos = own * MOBA_BLOCK + blk_offs
        s_own = jnp.where(k_pos[None, :] <= q_pos[:, None], s_own, -jnp.inf)
        p = jax.nn.softmax(jnp.concatenate([s_sel, s_own], axis=-1), axis=-1).astype(v_blocks.dtype)
        p_sel = p[..., :n_sel * MOBA_BLOCK].reshape(B, H, Q_CHUNK, n_sel, MOBA_BLOCK)
        p_own = p[..., n_sel * MOBA_BLOCK:]
        return (jnp.einsum('bhqjk,bhqjkd->bhqd', p_sel, vg)
                + jnp.einsum('bhqk,bhkd->bhqd', p_own, v_own))

    out = lax.map(chunk, jnp.arange(S // Q_CHUNK))
    return out.transpose(1, 0, 3, 2, 4).reshape(B, S, H * HEAD_DIM)

def second_inputs(seed: int = 0) -> dict:
    key = jax.random.key(seed)
    ks = jax.random.split(key, 10)
    f32 = jnp.float32
    nrm = jax.random.normal
    x = nrm(ks[0], (BATCH, SEQ, D_MODEL), f32)
    mem = nrm(ks[1], (BATCH, N_MEM, D_MODEL), f32)
    w_in = nrm(ks[2], (DEPTH_2, D_MODEL, IN_WIDTH), f32) * D_MODEL ** -0.5
    w_out = nrm(ks[3], (DEPTH_2, MIX_WIDTH, D_MODEL), f32) * (MIX_WIDTH ** -0.5 * DEEPNORM_BETA)
    w_mem_kv = nrm(ks[4], (DEPTH_2, D_MODEL, 2 * MEM_WIDTH), f32) * D_MODEL ** -0.5
    ln_g = 1.0 + 0.02 * nrm(ks[5], (DEPTH_2, D_MODEL), f32)
    ln_b = 0.02 * nrm(ks[6], (DEPTH_2, D_MODEL), f32)
    pool_w = nrm(ks[7], (N_A_LAYERS, N_POOL_GROUPS, POOL_GROUP, POOL_GROUP), f32) * POOL_GROUP ** -0.5
    pool_scale = 1.0 + 0.02 * nrm(ks[8], (N_A_LAYERS, BRANCH_WIDTH), f32)
    w_kv_shared = nrm(ks[9], (D_MODEL, 2 * BRANCH_WIDTH), f32) * D_MODEL ** -0.5
    return {"x": x, "mem": mem, "w_in": w_in, "w_out": w_out, "w_mem_kv": w_mem_kv,
            "ln_g": ln_g, "ln_b": ln_b, "pool_w": pool_w, "pool_scale": pool_scale,
            "w_kv_shared": w_kv_shared}

def second_block(x, mem, w_in, w_out, w_mem_kv, ln_g, ln_b, pool_w, pool_scale, w_kv_shared):
    h = x
    split_at = [BRANCH_WIDTH, 2 * BRANCH_WIDTH, 2 * BRANCH_WIDTH + MEM_WIDTH]
    for i in range(DEPTH_2):
        if i == N_A_LAYERS:
            k_blocks, v_blocks, k_mean = moba_shared_kv(h, w_kv_shared)
        u = h @ w_in[i]
        branch_in, gate_b, mem_q, gate_m = jnp.split(u, split_at, axis=-1)
        if i < N_A_LAYERS:
            branch = multiscale_pool(branch_in, pool_w[i], pool_scale[i])
        else:
            branch = moba_attention(branch_in, k_blocks, v_blocks, k_mean)
        mem_o = memory_attention(mem_q, mem, w_mem_kv[i])
        mixed = jnp.concatenate([branch * jax.nn.silu(gate_b), mem_o * jax.nn.silu(gate_m)], axis=-1)
        y = mixed @ w_out[i]
        h = layer_norm(DEEPNORM_ALPHA * h + y, ln_g[i], ln_b[i])
    return h


def setup_inputs(seed=0):
    out = dict(first_inputs(seed))
    for name, value in second_inputs(seed + 1).items():
        if name != "x":
            out[name + "_2"] = value
    return out


def reference(
    x, norm1_gain, w_in, hgrn_lb_param, hgrn_norm_gain, fox_gate_bias, w_out, norm2_gain,
    w_ffn_gate, w_ffn_up, ffn_conv_w, ffn_conv_b, w_ffn_down, final_norm_gain, mem_2, w_in_2,
    w_out_2, w_mem_kv_2, ln_g_2, ln_b_2, pool_w_2, pool_scale_2, w_kv_shared_2,
):
    x = first_block(
        x, norm1_gain, w_in, hgrn_lb_param, hgrn_norm_gain, fox_gate_bias, w_out, norm2_gain,
        w_ffn_gate, w_ffn_up, ffn_conv_w, ffn_conv_b, w_ffn_down, final_norm_gain,
    )
    return second_block(
        x, mem_2, w_in_2, w_out_2, w_mem_kv_2, ln_g_2, ln_b_2, pool_w_2, pool_scale_2,
        w_kv_shared_2,
    )


_drawn_inputs = setup_inputs


def setup_inputs(seed=0):
    import zlib

    import numpy as np

    out = dict(_drawn_inputs(seed))
    spreads = {}
    factors = {'norm1_gain': 2.711,
     'hgrn_norm_gain': 6.517,
     'fox_gate_bias': 3.856,
     'norm2_gain': 4.063,
     'ffn_conv_b': 6.037,
     'final_norm_gain': 2.738,
     'mem_2': 3.74,
     'w_mem_kv_2': 3.602,
     'pool_scale_2': 8.0}
    for name, (base, spread) in spreads.items():
        noise = np.random.default_rng([zlib.crc32(name.encode()), seed]).standard_normal(out[name].shape)
        drawn = base * np.exp(spread * noise) if base else spread * noise
        out[name] = __import__('jax').numpy.asarray(drawn.astype(out[name].dtype))
    for name, factor in factors.items():
        out[name] = (out[name] * factor).astype(out[name].dtype)
    return out
```

```python
import concourse.bass as bass
from concourse import mybir
from contextlib import ExitStack

F32 = mybir.dt.float32
F32R = mybir.dt.float32r
U32 = mybir.dt.uint32
ALU = mybir.AluOpType
ACT = mybir.ActivationFunctionType
AX = mybir.AxisListType

P = 128
TOK = 256
TT = TOK // P
D = 2048
KT = D // P
HG = 1024
HH = HG // P
CHUNK = 64
NCH = TOK // CHUNK
DFF = 5632
FB = DFF // P
HB = FB // 2
BR = 1536
BB = BR // P
MH = 4
PG = 3
WINDOWS = (2, 4, 8, 16)
PAD = 16
EPS = 1e-6
LN_EPS = 1e-5
ALPHA = (2 * 2) ** 0.25
SCALE = float(P) ** -0.5
NEG = -1e30
SLOT = 2048
ds = bass.ds


class Phase:

    def __init__(self, name, bodies, tpc, size, source, mats, form, rhs, first):
        self.name, self.bodies, self.tpc, self.size = name, bodies, tpc, size
        self.source, self.mats, self.form, self.rhs = source, mats, form, rhs
        self.tile0, self.chunk0 = first
        self.tpb = 2 * tpc
        self.end = (self.tile0 + bodies * self.tpb, self.chunk0 + bodies * 2)


def program(nc, A):
    ctx = ExitStack()
    with ctx:
        def sb(name, shape, dt=F32):
            return ctx.enter_context(nc.sbuf_tensor(name, shape, dt))

        def sem(name):
            return ctx.enter_context(nc.semaphore(name))

        ident = sb("ident", [P, P])
        meanw = sb("meanw", [P, P])
        maskneg = sb("maskneg", [P, P])
        tri01 = sb("tri01", [P, P])
        chunktri = sb("chunktri", [P, P])
        scanmask = sb("scanmask", [P, TOK])
        colv = sb("colv", [P, 321])
        convp = sb("convp", [P, FB, 4])
        convc = sb("convc", [P, 2, 4])
        epsr = sb("epsr", [P, 1])
        epsl = sb("epsl", [P, 1])
        one1 = sb("one1", [P, 1])
        invcnt = sb("invcnt", [P, PAD])
        lb = sb("lb", [P, HH])
        omlb = sb("omlb", [P, HH])
        lbt = sb("lbt", [P, 4, HH])
        decay = sb("decay", [P, HH, NCH])
        rstd = sb("rstd", [P, TOK])
        nmax = sb("nmax", [P, 2, TT])
        psumr = sb("psumr", [P, 2, TT])
        pinv = sb("pinv", [P, 2, TT])
        fbias = sb("fbias", [P, HH])
        fgate = sb("fgate", [P, TT, HH])
        fgt = sb("fgt", [P, 2, TT, HH])

        base = (nc.sbuf_base + 31) // 32 * 32
        ctx.enter_context(nc.sbuf_tensor("fence", [P, 200 * 256], F32))
        K = 1024

        def at(name, kib, shape, dt=F32):
            return nc.alloc_sbuf_tensor_at(name, shape, dt, offset=base + int(kib * K))

        raw = at("raw", 0, [P, 4, SLOT])
        hi = at("hi", 32, [P, 4, SLOT], F32R)
        lo = at("lo", 64, [P, 4, SLOT], F32R)
        xres = at("xres", 96, [P, KT, TOK])
        ah = at("ah", 112, [P, KT, TOK], F32R)
        al = at("al", 128, [P, KT, TOK], F32R)
        scr = at("scr", 112, [P, 4, SLOT])
        arena = at("arena", 144, [P, 7, SLOT])
        memtok = at("memtok", 112, [P, TT, D])
        xtok = at("xtok", 128, [P, TT, D])
        memh = at("memh", 144, [P, KT, TOK], F32R)
        meml = at("meml", 160, [P, KT, TOK], F32R)
        normt = at("normt", 176, [P, KT, TOK])
        vrows = at("vrows", 184, [P, 3, P])
        stage = at("stage", 192, [P, SLOT])
        fwraw = at("fwraw", 184, [P, KT, HH])
        fwhi = at("fwhi", 184.5, [P, KT, HH], F32R)
        fwlo = at("fwlo", 185, [P, KT, HH], F32R)
        hh = at("hh", 144, [P, HB, TOK], F32R)
        hl = at("hl", 144 + HB, [P, HB, TOK], F32R)
        cbuf = at("cbuf", 188, [P, 2, TOK])
        sbuf_ = at("silub", 190, [P, 2, TOK])
        hv = at("hv", 192, [P, 2, TOK])
        ph_ = at("pooledh", 176, [P, BB, TOK], F32R)
        pl_ = at("pooledl", 188, [P, BB, TOK], F32R)

        def blocks(t, n=8):
            return t.rearrange("p (b t) -> p b t", t=TOK)

        flat = arena[:, :, :].rearrange("p s n -> p (s n)")
        ablk = flat.rearrange("p (b t) -> p b t", t=TOK)
        sflat = scr[:, :, :].rearrange("p s n -> p (s n)")
        sblk = sflat.rearrange("p (b t) -> p b t", t=TOK)
        rflat = arena[:, :, :]

        G = ctx.enter_context(nc.psum_tensor("G", [P, 4, 512], F32))
        SB = ctx.enter_context(nc.psum_tensor("SB", [P, 2, 512], F32))
        TB = ctx.enter_context(nc.psum_tensor("TB", [P, 512], F32))
        OB = ctx.enter_context(nc.psum_tensor("OB", [P, 512], F32))
        XP = [SB[:, 0, :], SB[:, 1, :], TB[:, :], OB[:, :]]

        memkv = nc.dram_tensor("memkv_scratch", (2, P, SLOT), F32, kind="Internal").ap()

        raw_loaded = [sem(f"raw_loaded{s}") for s in range(4)]
        hi_ready, lo_ready, tile_used = sem("hi_ready"), sem("lo_ready"), sem("tile_used")
        pair_free = [sem("pair_free0"), sem("pair_free1")]
        consts = sem("consts")
        pool_seq = sem("pool_seq")
        vec_loaded, mem_loaded, x_loaded = sem("vec_loaded"), sem("mem_loaded"), sem("x_loaded")
        vec_t, vec_ready = sem("vec_t"), sem("vec_ready")
        in_t, mem_hi, mem_lo, x_ready = sem("in_t"), sem("mem_hi"), sem("mem_lo"), sem("x_ready")
        lb_chain = sem("lb_chain")
        lb_exp = sem("lb_exp")
        stored, reloaded, out_stored = sem("stored"), sem("reloaded"), sem("out_stored")
        n_mean, n_xc, n_sq, n_stat = sem("n_mean"), sem("n_xc"), sem("n_sq"), sem("n_stat")
        n_ln, n_rstd, n_y, n_b, n_hi, n_lo = (sem("n_ln"), sem("n_rstd"), sem("n_y"), sem("n_b"),
                                              sem("n_hi"), sem("n_lo"))
        fw_loaded, fb_loaded, fw_hi, fw_lo = sem("fw_loaded"), sem("fb_loaded"), sem("fw_hi"), sem("fw_lo")
        fg_done, fg_seq, fg_act, fc_done, fc_ready = (sem("fg_done"), sem("fg_seq"), sem("fg_act"),
                                                      sem("fc_done"), sem("fc_ready"))
        g_sig, g_seq, g_ln, g_act = sem("g_sig"), sem("g_seq"), sem("g_ln"), sem("g_act")
        r_a, r_kt, r_attn, r_kv, r_state, r_o, r_oev = (sem("r_a"), sem("r_kt"), sem("r_attn"),
                                                       sem("r_kv"), sem("r_state"), sem("r_o"), sem("r_oev"))
        r_sq, r_stat, r_ln, r_rstd, r_seq, r_hi = (sem("r_sq"), sem("r_stat"), sem("r_ln"), sem("r_rstd"),
                                                  sem("r_seq"), sem("r_hi"))
        conv_cur, conv_c, conv_1, conv_s, h_hi, h_lo = (
            sem("conv_cur"), sem("conv_c"), sem("conv_1"), sem("conv_s"), sem("h_hi"), sem("h_lo"))
        s_sc, s_mx, s_exp, s_inv, s_p, s_t, s_tc, s_o, s_tmp, s_hi, s_lo = (
            sem("s_scores"), sem("s_max"), sem("s_exp"), sem("s_inv"), sem("s_probs"), sem("s_probsT"),
            sem("s_probsT_sb"), sem("s_out"), sem("s_out_sb"), sem("s_out_hi"), sem("s_out_lo"))
        silu_done, p_seq, p_hi, p_lo = sem("silu_done"), sem("p_seq"), sem("p_hi"), sem("p_lo")
        pm_h, pm_l = sem("pm_hi"), sem("pm_lo")
        o_t, o_sb = sem("o_t"), sem("o_sb")
        q_scaled = sem("q_scaled")
        b_val, b_hi, b_lo = sem("b_value"), sem("b_hi"), sem("b_lo")

        def kview(w):
            return w.rearrange("(t p) n -> p t n", p=P)

        def std(w, col, cols_of_body=512):
            v = kview(w)

            def source(i, j):
                return v[:, (j % 2) * 8:(j % 2) * 8 + 8, ds(i * cols_of_body + (col + (j // 2) * 256), 256)]
            return source

        def ffn_source(half):
            vg, vu = kview(A["w_ffn_gate"]), kview(A["w_ffn_up"])

            def source(i, j):
                v = vg if j < 2 else vu
                return v[:, (j % 2) * 8:(j % 2) * 8 + 8, ds(i * 256 + half * HB * P, 256)]
            return source

        def down_source(half):
            v = kview(A["w_ffn_down"])

            def source(i, j):
                t = half * HB + (j % 2) * (HB // 2)
                return v[:, t:t + HB // 2, ds(i * 512 + (j // 2) * P, P)]
            return source

        def pool_source(i, j):
            b = i * 4 + j
            return A["pool_w"][b // PG].rearrange("(t p) n -> p t n", p=P)[:, :, (b % PG) * P:(b % PG + 1) * P]

        def std_mats(i, j):
            return [(b, [(k, (j % 2) * 8 + k) for k in range(8)], 256, b * P, j % 2 == 0, j % 2 == 1) for b in (0, 1)]

        def down_mats(i, j):
            n = HB // 2
            return [((j // 2) % 2, [(k, (j % 2) * n + k) for k in range(n)], P, 0, j % 2 == 0, j % 2 == 1)]

        def pool_mats(i, j):
            b = i * 4 + j
            return [(j % 2, [(k, b // PG * PG + k) for k in range(PG)], P, 0, True, True)]

        phases = {}
        at_ = [(0, 0)]

        def add(name, bodies, source, rhs, form="A", tpc=2, size=SLOT, mats=std_mats):
            p = phases[name] = Phase(name, bodies, tpc, size, source, mats, form, rhs, at_[0])
            at_[0] = p.end

        mem_ops, act_ops, h_ops, pool_ops = (memh, meml), (ah, al), (hh, hl), (ph_, pl_)
        for l in range(2):
            add(f"mem_k{l}", 1, std(A["w_mem_kv"][l], 0), mem_ops)
            add(f"mem_v{l}", 1, std(A["w_mem_kv"][l], 512), mem_ops, form="B")
        add("in_qf", 4, std(A["w_in"], 0), act_ops)
        add("in_i", 2, std(A["w_in"], 2 * HG), act_ops, form="B")
        add("in_gqk", 6, std(A["w_in"], 3 * HG), act_ops)
        add("in_v", 2, std(A["w_in"], 6 * HG), act_ops, form="B")
        add("out", 4, std(A["w_out"], 0), act_ops)
        for half in range(2):
            add(f"ffn{half}", HB // 2, ffn_source(half), act_ops)
            add(f"down{half}", 4, down_source(half), h_ops, tpc=4, size=HB // 2 * P, mats=down_mats)
        add("in0_branch", 3, std(A["w_in_2"][0], 0), act_ops)
        add("in0_gate", 3, std(A["w_in_2"][0], BR), act_ops)
        add("in0", 2, std(A["w_in_2"][0], 2 * BR), act_ops)
        add("pool", 3, pool_source, pool_ops, size=PG * P, mats=pool_mats)
        add("out0", 4, std(A["w_out_2"][0], 0), act_ops)
        add("kvs_k", 3, std(A["w_kv"], 0), act_ops)
        add("kvs_v", 3, std(A["w_kv"], BR), act_ops, form="B")
        add("in1_q", 3, std(A["w_in_2"][1], 0), act_ops)
        add("in1_gate", 3, std(A["w_in_2"][1], BR), act_ops)
        add("in1", 2, std(A["w_in_2"][1], 2 * BR), act_ops)
        add("out1", 4, std(A["w_out_2"][1], 0), act_ops)
        order = list(phases.values())
        follow = {p.name: q for p, q in zip(order, order[1:])}

        def tile_wait(eng, sm, value):
            if not isinstance(value, int) or value > 0:
                eng.wait_ge(sm, value)

        def sized(t, s, size):
            return t[:, s, 0:size]

        def sp_phase(eng, name):
            p = phases[name]

            def body(i):
                for j in range(p.tpb):
                    n = i * p.tpb + (p.tile0 + j)
                    tile_wait(eng, lo_ready, n - 3)
                    src = p.source(i, j)
                    dst = sized(raw, j % 4, p.size).rearrange("p (t n) -> p t n", t=src.shape[1])
                    eng.dma_start(dst, src).then_inc(raw_loaded[j % 4], 16)
            loop(eng, p.bodies, body, p.name == "pool")

        def loop(eng, n, body, unroll=False):
            if n == 1 or unroll:
                for i in range(n):
                    body(i)
            else:
                with eng.Fori(0, n) as i:
                    body(i)

        def splits(eng, act, p, i, first, count=None):
            for j in range(first, first + (count or p.tpc)):
                s = j % 4
                n = i * p.tpb + (p.tile0 + j)
                if act:
                    eng.wait_ge(raw_loaded[s], (i * p.tpb + (p.tile0 + j - s)) * 4 + 16)
                    tile_wait(eng, tile_used, n - 3)
                    eng.activation(sized(hi, s, p.size), sized(raw, s, p.size), ACT.Copy).then_inc(hi_ready, 1)
                else:
                    eng.wait_ge(hi_ready, n + 1)
                    eng.tensor_tensor(sized(lo, s, p.size), sized(raw, s, p.size),
                                      sized(hi, s, p.size).bitcast(F32), ALU.subtract).then_inc(lo_ready, 1)

        def cut_phase(eng, act, name, evict, between=None):
            p = phases[name]

            def body(i, nxt, ni):
                if between is not None:
                    splits(eng, act, p, i, 2, 1)
                    between(4 * i)
                    splits(eng, act, p, i, 3, 1)
                    between(4 * i + 1)
                    evict(i, 0)
                    splits(eng, act, nxt, ni, 0, 1)
                    between(4 * i + 2)
                    splits(eng, act, nxt, ni, 1, 1)
                    between(4 * i + 3)
                    evict(i, 1)
                    return
                splits(eng, act, p, i, p.tpc)
                evict(i, 0)
                if nxt is not None:
                    splits(eng, act, nxt, ni, 0)
                evict(i, 1)
            if p.bodies > 1:
                loop(eng, p.bodies - 1, lambda i: body(i, p, i + 1), p.name == "pool" or between is not None)
            body(p.bodies - 1, follow.get(name), 0)

        def no_evict(i, cb):
            pass

        def pe_phase(eng, name, between=None, norm=None):
            p = phases[name]
            xh, xl = p.rhs

            def body(i):
                for j in range(p.tpb):
                    s, cb = j % 4, j // p.tpc
                    eng.wait_ge(lo_ready, i * p.tpb + (p.tile0 + j + 1))
                    if norm is not None:
                        eng.wait_ge(n_lo, 4 * norm + 2 + 2 * (j % 2))
                    if j % p.tpc == 0:
                        tile_wait(eng, pair_free[cb], i + p.chunk0 // 2)
                    if name.startswith("down") and j < 2:
                        half = int(name[-1])
                        eng.wait_ge(h_lo, HB // 2 * half + (6 if j == 0 else 11))
                    last = None
                    for b, ks, width, col, first, final in p.mats(i, j):
                        bank = 2 * cb + b
                        for q, (kt, k) in enumerate(ks):
                            st, sp = first and q == 0, final and q == len(ks) - 1
                            if p.form == "A":
                                w = slice(kt * width + col, kt * width + col + P)
                                wh, wl = hi[:, s, w], lo[:, s, w]
                                pairs = [(wh, xh[:, k, :]), (wh, xl[:, k, :]), (wl, xh[:, k, :])]
                            else:
                                w = slice(kt * width, (kt + 1) * width)
                                wh, wl = hi[:, s, w], lo[:, s, w]
                                t = slice(b * P, (b + 1) * P)
                                pairs = [(xh[:, k, t], wh), (xh[:, k, t], wl), (xl[:, k, t], wh)]
                            for r, (l_, r_) in enumerate(pairs):
                                last = eng.matmul(G[:, bank, 0:256], l_, r_, start=st and r == 0, stop=sp and r == 2)
                    last.then_inc(tile_used, 1)
                    if between is not None:
                        between(4 * i + j)
            loop(eng, p.bodies, body, p.name == "pool" or between is not None)

        def chunk_wait(eng, p, i, cb):
            eng.wait_ge(tile_used, i * p.tpb + (p.tile0 + (cb + 1) * p.tpc))

        def left_wait(eng, p, i, cb):
            eng.wait_ge(pair_free[cb], i + (p.chunk0 // 2 + 1))

        def copy_evict(eng, name, block0):
            p = phases[name]

            def evict(i, cb):
                chunk_wait(eng, p, i, cb)
                eng.activation(ablk[:, ds(i * 4 + (block0 + 2 * cb), 2), :], G[:, 2 * cb:2 * cb + 2, 0:256],
                               ACT.Copy).then_inc(pair_free[cb], 1)
            return evict

        def token_evict(eng, name, dst):
            p = phases[name]

            def evict(i, cb):
                chunk_wait(eng, p, i, cb)
                eng.activation(dst[:, :, ds(i * 512 + cb * 256, 256)], G[:, 2 * cb:2 * cb + 2, 0:256],
                               ACT.Copy).then_inc(pair_free[cb], 1)
            return evict

        def residual_evict(eng, name, alpha=None):
            p = phases[name]

            def evict(i, cb):
                chunk_wait(eng, p, i, cb)
                x = xres[:, ds(i * 4 + 2 * cb, 2), :]
                g = G[:, 2 * cb:2 * cb + 2, 0:256]
                if alpha is None:
                    ins = eng.tensor_tensor(x, x, g, ALU.add)
                else:
                    ins = eng.scalar_tensor_tensor(x, x, alpha, g, ALU.mult, ALU.add)
                ins.then_inc(pair_free[cb], 1)
            return evict

        def phase_over(eng, name):
            n = phases[name].end[1] // 2
            eng.wait_ge(pair_free[0], n)
            eng.wait_ge(pair_free[1], n)

        NORMS = {0: (0, None, normt), 1: (16, None, normt), 2: (32, None, xres), 3: (48, 80, xres), 4: (64, 96, xres)}

        def quarter(t, q):
            return t[:, 4 * q:4 * q + 4, :]

        def pe_norm(eng, u):
            if u >= 3:
                for k in range(KT):
                    last = eng.matmul(OB[:, 0:TOK], meanw[:, :], xres[:, k, :], start=k == 0, stop=k == KT - 1)
                last.then_inc(n_mean, 1)
            for k in range(KT):
                if k % 4 == 0:
                    eng.wait_ge(n_sq, 4 * u + k // 4 + 1)
                last = eng.matmul(TB[:, 0:TOK], meanw[:, :], normt[:, k, :], start=k == 0, stop=k == KT - 1)
            last.then_inc(n_stat, 1)

        def act_norm_squares(eng, u):
            for q in range(4):
                if u >= 3:
                    eng.wait_ge(n_xc, 4 * (u - 3) + q + 1)
                eng.activation(quarter(normt, q), quarter(xres, q), ACT.Square).then_inc(n_sq, 1)

        def act_norm_scale(eng, u):
            eng.wait_ge(n_stat, u + 1)
            eng.activation(rstd[:, :], TB[:, 0:TOK], ACT.Ln, bias=(epsl if u >= 3 else epsr)[:, 0:1]).then_inc(n_ln, 1)
            eng.wait_ge(n_ln, u + 1)
            eng.activation(rstd[:, :], rstd[:, :], ACT.Exp, scale=-0.5).then_inc(n_rstd, 1)

        def act_norm_out(eng, u, split=True):
            gain, bias, dst = NORMS[u]
            for q in range(4):
                eng.wait_ge(n_y, 4 * u + q + 1)
                if bias is not None:
                    for k in range(4 * q, 4 * q + 4):
                        ins = eng.activation(dst[:, k, :], dst[:, k, :], ACT.Identity, bias=colv[:, bias + k:bias + k + 1])
                    ins.then_inc(n_b, 1)
                    eng.wait_ge(n_b, 4 * (u - 3) + q + 1)
                if split:
                    eng.activation(quarter(ah, q), quarter(dst, q), ACT.Copy).then_inc(n_hi, 1)

        def dve_norm(eng, u, split=True):
            gain, bias, dst = NORMS[u]
            if u >= 3:
                eng.wait_ge(n_mean, u - 2)
                for q in range(4):
                    eng.tensor_tensor(quarter(xres, q), quarter(xres, q),
                                      OB[:, 0:TOK].unsqueeze(1).broadcast_to([P, 4, TOK]), ALU.subtract).then_inc(n_xc, 1)
                eng.wait_ge(n_xc, 4 * (u - 2))
            eng.wait_ge(n_rstd, u + 1)
            for q in range(5):
                if q < 4:
                    for k in range(4 * q, 4 * q + 4):
                        ins = eng.scalar_tensor_tensor(dst[:, k, :], xres[:, k, :], colv[:, gain + k:gain + k + 1],
                                                       rstd[:, :], ALU.mult, ALU.mult)
                    ins.then_inc(n_y, 1)
                if split and q > 0:
                    eng.wait_ge(n_hi, 4 * u + q)
                    eng.tensor_tensor(quarter(al, q - 1), quarter(dst, q - 1), quarter(ah, q - 1).bitcast(F32),
                                      ALU.subtract).then_inc(n_lo, 1)

        class Heads:

            def __init__(self, first, n, q, k, v, causal, out0, probs, gate=None, forget=False, cut=0):
                self.cut = cut
                self.first, self.n, self.q, self.k, self.v = first, n, q, k, v
                self.causal, self.out0, self.gate, self.forget = causal, out0, gate, forget
                self.p = [probs[:, 0:512].rearrange("p (a b) -> p a b", a=2),
                          probs[:, 512:1024].rearrange("p (a b) -> p a b", a=2)]
                self.t = [probs[:, 1024:1536], probs[:, 1536:2048]]

        fcT = ablk[:, 8, :]
        fcN = ablk[:, 9, :]
        flf = ablk[:, 10, :].rearrange("p (a b) -> p a b", a=2)

        def pe_heads(eng, H, first=0, end=None):
            for step in range(first, end or H.n + 2):
                h = step
                if h < H.n:
                    g = H.first + h
                    if g >= 2:
                        eng.wait_ge(s_exp, g - 1)
                    for qt in range(TT):
                        nk = P * (qt + 1) if H.causal else TOK
                        out = SB[:, g % 2, qt * TOK:qt * TOK + nk]
                        mm = [(H.q(h)[:, qt * P:(qt + 1) * P], H.k(h)[:, 0:nk], out)]
                        if H.forget:
                            mm.append((fcT[:, qt * P:(qt + 1) * P], ident[:, h:h + 1].to_broadcast([P, nk]), out))
                            mm.append((ident[:, h:h + 1].to_broadcast([P, P]), fcN[:, 0:nk], out))
                        if H.causal:
                            mm.append((ident[:, :], maskneg[:, :], SB[:, g % 2, qt * TOK + nk - P:qt * TOK + nk]))
                        for m, (l_, r_, o_) in enumerate(mm):
                            last = eng.matmul(o_, l_, r_, start=m == 0, stop=m == len(mm) - 1)
                    last.then_inc(s_sc, 1)
                h = step - 1
                if 0 <= h < H.n:
                    g = H.first + h
                    eng.wait_ge(s_p, g + 1)
                    if g >= 1:
                        eng.wait_ge(s_tc, g)
                    pr = H.p[h % 2]
                    eng.transpose(TB[:, 0:128], pr[:, 0, 0:128], ident[:, :])
                    eng.transpose(TB[:, 128:256], pr[:, 1, 0:128], ident[:, :])
                    if not H.causal:
                        eng.transpose(TB[:, 384:512], pr[:, 0, 128:256], ident[:, :])
                    eng.transpose(TB[:, 256:384], pr[:, 1, 128:256], ident[:, :]).then_inc(s_t, 1)
                h = step - 2
                if 0 <= h < H.n:
                    g = H.first + h
                    eng.wait_ge(s_tc, g + 1)
                    if g >= 1:
                        eng.wait_ge(s_tmp, g)
                    pt = H.t[h % 2]
                    eng.matmul(OB[:, 0:256], H.v(h, 0), pt[:, 0:256], start=True, stop=False)
                    if not H.causal:
                        eng.matmul(OB[:, 0:128], H.v(h, 1), pt[:, 384:512], start=False, stop=False)
                    eng.matmul(OB[:, 128:256], H.v(h, 1), pt[:, 256:384], start=False, stop=True).then_inc(s_o, 1)

        def act_heads(eng, H, first=0, end=None):
            for step in range(first, end or H.n + 2):
                h = step
                if h < H.n:
                    g = H.first + h
                    eng.wait_ge(s_mx, g + 1)
                    if h >= 2:
                        eng.wait_ge(s_t, g - 1)
                    for qt in range(TT):
                        nk = P * (qt + 1) if H.causal else TOK
                        ins = eng.activation(H.p[h % 2][:, qt, 0:nk], SB[:, g % 2, qt * TOK:qt * TOK + nk], ACT.Exp,
                                             bias=nmax[:, g % 2, qt:qt + 1], accum_out=psumr[:, g % 2, qt:qt + 1])
                    ins.then_inc(s_exp, 1)
                h = step - 1
                if 0 <= h < H.n:
                    g = H.first + h
                    eng.wait_ge(s_t, g + 1)
                    if h >= 2:
                        eng.wait_ge(s_o, g - 1)
                    n = 384 if H.causal else 512
                    eng.activation(H.t[h % 2][:, 0:n], TB[:, 0:n], ACT.Copy).then_inc(s_tc, 1)
                h = step - 2
                if 0 <= h < H.n:
                    g = H.first + h
                    if H.out0 is None:
                        continue
                    eng.wait_ge(s_tmp, g + 1)
                    eng.activation(ah[:, H.out0 + h, :], rstd[:, :], ACT.Copy).then_inc(s_hi, 1)

        def dve_heads(eng, H, first=0, end=None):
            for step in range(first, end or H.n + 2):
                h = step
                if h < H.n:
                    g = H.first + h
                    eng.wait_ge(s_sc, g + 1)
                    if g >= 2:
                        eng.wait_ge(s_exp, g - 1)
                    for qt in range(TT):
                        nk = P * (qt + 1) if H.causal else TOK
                        ins = eng.tensor_reduce(nmax[:, g % 2, qt:qt + 1], SB[:, g % 2, qt * TOK:qt * TOK + nk],
                                                AX.X, ALU.max, negate=True)
                    ins.then_inc(s_mx, 1)
                h = step - 1
                if 0 <= h < H.n:
                    g = H.first + h
                    eng.wait_ge(s_exp, g + 1)
                    eng.reciprocal(pinv[:, g % 2, :], psumr[:, g % 2, :]).then_inc(s_inv, 1)
                    eng.wait_ge(s_inv, g + 1)
                    for qt in range(TT):
                        nk = P * (qt + 1) if H.causal else TOK
                        pr = H.p[h % 2][:, qt, 0:nk]
                        ins = eng.tensor_scalar(pr, pr, pinv[:, g % 2, qt:qt + 1], None, ALU.mult)
                    ins.then_inc(s_p, 1)
                h = step - 2
                if 0 <= h < H.n:
                    g = H.first + h
                    eng.wait_ge(s_o, g + 1)
                    if H.out0 is None:
                        eng.tensor_copy(H.q(h), OB[:, 0:256]).then_inc(s_tmp, 1)
                        continue
                    if h >= 1:
                        eng.wait_ge(s_lo, H.cut + h)
                    if H.gate is None:
                        ins = eng.tensor_copy(rstd[:, :], OB[:, 0:256])
                    else:
                        ins = eng.tensor_tensor(rstd[:, :], OB[:, 0:256], H.gate(h), ALU.mult)
                    ins.then_inc(s_tmp, 1)
                    eng.wait_ge(s_hi, H.cut + h + 1)
                    eng.tensor_tensor(al[:, H.out0 + h, :], rstd[:, :], ah[:, H.out0 + h, :].bitcast(F32),
                                      ALU.subtract).then_inc(s_lo, 1)

        def tok_v(t):
            return lambda h, kt: t[:, kt, h * P:(h + 1) * P]

        slot_tok = lambda s, n: rflat[:, s, :].rearrange("p (a n) -> p a n", a=2)
        fox = Heads(0, HH, lambda h: ablk[:, 32 + h, :], lambda h: ablk[:, 40 + h, :], tok_v(slot_tok(6, HG)),
                    True, HH, flat[:, 0:SLOT], forget=True)
        memA = flat[:, 0:SLOT]
        heads_a = Heads(8, MH, lambda h: ablk[:, 24 + h, :], lambda h: memA[:, h * TOK:(h + 1) * TOK],
                        tok_v(memA[:, 1024:2048].rearrange("p (a n) -> p a n", a=2)),
                        False, BB, flat[:, 32 * TOK:32 * TOK + SLOT], gate=lambda h: ablk[:, 28 + h, :], cut=8)
        memB = sflat[:, 0:SLOT]
        heads_b = Heads(24, MH, lambda h: ablk[:, 48 + h, :], lambda h: memB[:, h * TOK:(h + 1) * TOK],
                        tok_v(memB[:, 1024:2048].rearrange("p (a n) -> p a n", a=2)),
                        False, BB, sflat[:, 16 * TOK:16 * TOK + SLOT], gate=lambda h: ablk[:, 52 + h, :], cut=12)
        vshared = flat[:, 12 * TOK:24 * TOK].rearrange("p (a n) -> p a n", a=2)
        moba = Heads(12, BB, lambda h: ablk[:, 24 + h, :], lambda h: ablk[:, h, :], tok_v(vshared),
                     True, None, flat[:, 48 * TOK:48 * TOK + SLOT])

        W = PAD + TOK
        pads = [flat[:, 24 * TOK + b * PG * W:24 * TOK + (b + 1) * PG * W].rearrange("p (a t) -> p a t", a=PG)
                for b in range(2)]

        def pool_out(g):
            return pads[g % 2][:, :, PAD:W]

        T = [scr[:, s, :] for s in range(4)]
        V_TOK = slot_tok(2, HG)

        def head(t, h):
            return t[:, h * TOK:(h + 1) * TOK]

        attn_sb = [T[0][:, 256 * b:256 * b + 256] for b in range(2)]
        kend_sb = [T[0][:, 512 + 384 * b:896 + 384 * b] for b in range(2)]
        state = [T[0][:, 1280 + 384 * b:1664 + 384 * b].rearrange("p (a b) -> p a b", a=3) for b in range(2)]
        QD, KE, GS, OUT = rflat[:, 0, :], rflat[:, 1, :], rflat[:, 3, :], rflat[:, 0, :]
        KD = T[3]

        block = ctx.enter_context(nc.Block())

        @block.sync
        def _(sp):
            rows = ((A["norm1"], 0, 0, 16), (A["norm2"], 0, 16, 16), (A["final"], 0, 32, 16), (A["ln_g"], 0, 48, 32),
                    (A["ln_b"], 0, 80, 32), (A["pool_scale"], 0, 112, 12), (A["conv_w"][0:2], 1, 0, 88),
                    (A["lbp"], 1, 88, 16), (A["hgain"], 1, 104, 1), (A["conv_w"][2:3], 2, 0, 44), (A["conv_b"], 2, 44, 44))
            for j in range(2):
                sp.dma_start(memtok[:, j, :], A["mem"][j * P:(j + 1) * P, :]).then_inc(mem_loaded, 16)
            for v, tile, r0, n in rows:
                src = v.rearrange("a (r p) -> (a r) p", p=P)
                sp.dma_start(vrows[r0:r0 + n, tile, :], src).then_inc(vec_loaded, 16)
            sp_phase(sp, "mem_k0")
            for j in range(2):
                sp.dma_start(xtok[:, j, :], A["x"][j * P:(j + 1) * P, :]).then_inc(x_loaded, 16)
            for p in order[1:]:
                sp_phase(sp, p.name)
            for j in range(TT):
                sp.wait_ge(o_sb, 4 * (j + 1))
                sp.dma_start(A["result"][j * P:(j + 1) * P, :], sflat[:, j * D:(j + 1) * D]).then_inc(out_stored, 16)
            sp.wait_ge(out_stored, 32)

        @block.gpsimd
        def _(pool):
            count = [0]

            def link(ins):
                count[0] += 1
                ins.then_inc(pool_seq, 1)
                pool.wait_ge(pool_seq, count[0])

            link(pool.memset(meanw[:, :], 1.0 / D))
            link(pool.memset(epsr[:, :], EPS))
            link(pool.memset(epsl[:, :], LN_EPS))
            link(pool.memset(one1[:, :], 1.0))
            for t in range(PAD):
                link(pool.memset(invcnt[:, t:t + 1], 1.0 / (t + 1)))
            link(pool.memset(maskneg[:, :], 0.0))
            link(pool.memset(tri01[:, :], 1.0))
            link(pool.memset(scanmask[:, :], 1.0))
            link(pool.memset(scanmask[:, :].rearrange("p (n c) -> p n c", c=CHUNK)[:, :, 0:1], 0.0))
            link(pool.memset(ident[:, :], 0.0))
            link(pool.affine_select(out=maskneg[:, :], in_=maskneg[:, :], compare_op=ALU.is_ge, fill=NEG, base=0,
                                    pattern=[[-1, P]], channel_multiplier=1))
            link(pool.affine_select(out=tri01[:, :], in_=tri01[:, :], compare_op=ALU.is_ge, fill=0.0, base=0,
                                    pattern=[[1, P]], channel_multiplier=-1))
            link(pool.tensor_copy(chunktri[:, :], tri01[:, :]))
            link(pool.memset(chunktri[0:CHUNK, CHUNK:P], 0.0))
            pool.affine_select(out=ident[:, :], in_=ident[:, :], compare_op=ALU.not_equal, fill=1.0, base=0,
                               pattern=[[-1, P]], channel_multiplier=1).then_inc(consts, 1)
            pool.dma_start(fbias[:, :], A["fox_bias"].to_broadcast([P, HH])).then_inc(fb_loaded, 16)
            for l in range(2):
                phase_over(pool, f"mem_v{l}")
                pool.dma_start(memkv[l], stage[:, :]).then_inc(stored, 16)
            pool.wait_ge(n_lo, 4)
            pool.dma_start(fwraw[:, :, :], A["w_in"][:, 7 * HG:7 * HG + HH].rearrange("(t p) n -> p t n", p=P))\
                .then_inc(fw_loaded, 16)
            pool.wait_ge(stored, 32)
            pool.wait_ge(p_lo, 4)
            pool.dma_start(memA, memkv[0]).then_inc(reloaded, 16)
            pool.wait_ge(tile_used, phases["in1"].end[0])
            pool.dma_start(memB, memkv[1]).then_inc(reloaded, 16)

        @block.tensor
        def _(pe):
            pe.wait_ge(consts, 1)
            turn = 0

            def transposes(src, loaded, done_sems):
                nonlocal turn
                for g in range(8):
                    if turn >= 4:
                        prev = turn - 4
                        if prev < 8:
                            pe.wait_ge(mem_lo, prev + 1)
                        else:
                            pe.wait_ge(x_ready, prev - 7)
                    for k in range(2):
                        for t in range(TT):
                            kk = 2 * g + k
                            last = pe.transpose(XP[turn % 4][:, k * 256 + t * P:k * 256 + (t + 1) * P],
                                                src[:, t, kk * P:(kk + 1) * P], ident[:, :])
                    last.then_inc(in_t, 1)
                    turn += 1

            pe.wait_ge(mem_loaded, 32)
            transposes(memtok, None, None)
            pe.wait_ge(x_loaded, 32)
            transposes(xtok, None, None)
            pe.wait_ge(vec_loaded, 11 * 16)
            pe.wait_ge(x_ready, 5)
            for v, n in enumerate((124, 105, 88)):
                last = pe.transpose(XP[0][:, v * P:v * P + n], vrows[0:n, v, :], ident[0:n, 0:n])
            last.then_inc(vec_t, 1)
            pe.wait_ge(mem_lo, 8)
            pe_phase(pe, "mem_k0")
            pe.wait_ge(x_ready, 8)
            pe_norm(pe, 0)
            for n in ("mem_v0", "mem_k1", "mem_v1"):
                pe_phase(pe, n)
            pe_phase(pe, "in_qf", norm=0)
            pe.wait_ge(fw_lo, 1)
            for t in range(TT):
                for k in range(KT):
                    x_h, x_l = ah[:, k, t * P:(t + 1) * P], al[:, k, t * P:(t + 1) * P]
                    for r, (l_, r_) in enumerate(((x_h, fwhi[:, k, :]), (x_h, fwlo[:, k, :]), (x_l, fwhi[:, k, :]))):
                        last = pe.matmul(TB[:, t * HH:(t + 1) * HH], l_, r_, start=k == 0 and r == 0,
                                         stop=k == KT - 1 and r == 2)
            last.then_inc(fg_done, 1)
            for n in ("in_i", "in_gqk", "in_v"):
                pe_phase(pe, n)
            pe.wait_ge(r_attn, 1)
            phase_over(pe, "in_v")
            for step in range(HH + 2):
                h = step
                if h < HH:
                    if h >= 2:
                        pe.wait_ge(r_attn, h)
                    bank = SB[:, h % 2, :]
                    for t in range(TT):
                        c = slice(t * P, (t + 1) * P)
                        pe.matmul(bank[:, t * P:(t + 1) * P], head(KD, h)[:, c], head(QD, h)[:, c], start=True, stop=True)
                        last = pe.transpose(bank[:, 256 + t * P:256 + (t + 1) * P], head(KE, h)[:, c], ident[:, :])
                    last.then_inc(r_a, 1)
                h = step - 1
                if 0 <= h < HH:
                    pe.wait_ge(r_kt, h + 1)
                    if h >= 1:
                        pe.wait_ge(r_state, 3 * h)
                    for n in range(NCH - 1):
                        c = (0, 2, 1)[n] * P
                        last = pe.matmul(TB[:, n * P:(n + 1) * P], kend_sb[h % 2][:, c:c + P],
                                         V_TOK[:, n // 2, h * P:(h + 1) * P], start=True, stop=True)
                    last.then_inc(r_kv, 1)
                h = step - 2
                if 0 <= h < HH:
                    pe.wait_ge(r_state, 3 * (h + 1))
                    pe.wait_ge(r_attn, h + 2)
                    if h >= 1:
                        pe.wait_ge(r_oev, h)
                    for t in range(TT):
                        pe.matmul(OB[:, t * P:(t + 1) * P], V_TOK[:, t, h * P:(h + 1) * P],
                                  attn_sb[h % 2][:, t * P:(t + 1) * P], start=True, stop=False)
                        for n in range(max(1, 2 * t), 2 * t + 2):
                            c = slice(n * CHUNK, (n + 1) * CHUNK)
                            last = pe.matmul(OB[:, c], state[h % 2][:, n - 1, :], head(QD, h)[:, c],
                                             start=False, stop=n % 2 == 1)
                    last.then_inc(r_o, 1)
            pe.wait_ge(r_sq, 1)
            for b in range(4):
                pe.matmul(G[:, b, :], meanw[:, :], T[2][:, b * 512:(b + 1) * 512], start=True, stop=True)\
                    .then_inc(r_stat, 1)
            pe.wait_ge(fg_seq, 7)
            pe.matmul(TB[:, 0:P], flf[:, 0, :], tri01[:, :], start=True, stop=True)
            pe.matmul(TB[:, P:2 * P], flf[:, 0, :], meanw[:, :], start=True, stop=True).then_inc(fc_done, 1)
            pe.wait_ge(r_oev, HH)
            pe.matmul(OB[:, 0:P], flf[:, 1, :], tri01[:, :], start=True, stop=True).then_inc(fc_done, 1)
            pe.wait_ge(fc_ready, 4)
            pe_heads(pe, fox)
            pe.wait_ge(s_lo, 8)
            pe.wait_ge(r_hi, 2)
            pe_phase(pe, "out")
            phase_over(pe, "out")
            pe_norm(pe, 1)
            for half in range(2):
                pe_phase(pe, f"ffn{half}", norm=1)
                pe_phase(pe, f"down{half}")
            phase_over(pe, "down1")
            pe_norm(pe, 2)
            for n in ("in0_branch", "in0_gate", "in0"):
                pe_phase(pe, n, norm=2)
            pe.wait_ge(p_lo, 4)
            pe_phase(pe, "pool")
            pe.wait_ge(reloaded, 16)
            pe.wait_ge(pm_l, 6)
            pe.wait_ge(q_scaled, 1)
            pe_heads(pe, heads_a)
            pe.wait_ge(s_lo, 12)
            pe_phase(pe, "out0")
            phase_over(pe, "out0")
            pe_norm(pe, 3)
            for n in ("kvs_k", "kvs_v", "in1_q"):
                pe_phase(pe, n, norm=3)
            phase_over(pe, "in1_q")
            pe.wait_ge(q_scaled, 2)
            pe_phase(pe, "in1_gate", between=lambda m: pe_heads(pe, moba, m, m + 1))
            pe_heads(pe, moba, BB)
            pe_phase(pe, "in1")
            pe.wait_ge(reloaded, 32)
            pe.wait_ge(q_scaled, 3)
            pe_heads(pe, heads_b)
            pe.wait_ge(s_lo, 16)
            pe.wait_ge(b_lo, 4)
            pe_phase(pe, "out1")
            phase_over(pe, "out1")
            pe_norm(pe, 4)
            for t in range(TT):
                for q in range(4):
                    n = 4 * t + q
                    if t == 0:
                        pe.wait_ge(n_b, 4 + q + 1)
                    if n >= 4:
                        pe.wait_ge(o_sb, n - 3)
                    for k in range(4):
                        last = pe.transpose(G[:, n % 4, k * P:(k + 1) * P], xres[:, 4 * q + k, t * P:(t + 1) * P], ident[:, :])
                    last.then_inc(o_t, 1)

        @block.scalar
        def _(act):
            splits(act, True, order[0], 0, 0)
            for g in range(8):
                act.wait_ge(in_t, g + 1)
                act.activation(memh[:, 2 * g:2 * g + 2, :], blocks(XP[g % 4]), ACT.Copy).then_inc(mem_hi, 1)
            for g in range(8):
                act.wait_ge(in_t, g + 9)
                act.activation(xres[:, 2 * g:2 * g + 2, :], blocks(XP[g % 4]), ACT.Copy).then_inc(x_ready, 1)
            act.wait_ge(x_ready, 8)
            act.wait_ge(vec_t, 1)
            act_norm_squares(act, 0)

            def kv_evict(name, token):
                p = phases[name]

                def evict(i, cb):
                    chunk_wait(act, p, i, cb)
                    if name in ("mem_k1",):
                        act.wait_ge(stored, 16)
                    if token:
                        dst = stage[:, 1024:2048].rearrange("p (a n) -> p a n", a=2)[:, :, cb * 256:(cb + 1) * 256]
                    else:
                        dst = blocks(stage[:, cb * 512:(cb + 1) * 512])
                    act.activation(dst, G[:, 2 * cb:2 * cb + 2, 0:256], ACT.Copy).then_inc(pair_free[cb], 1)
                return evict

            cut_phase(act, True, "mem_k0", kv_evict("mem_k0", False))
            act_norm_scale(act, 0)
            act_norm_out(act, 0)
            act.wait_ge(lb_chain, 3)
            act.activation(lbt[:, 2:4, :], lbt[:, 0:2, :], ACT.Exp).then_inc(lb_exp, 1)
            cut_phase(act, True, "mem_v0", kv_evict("mem_v0", True))
            cut_phase(act, True, "mem_k1", kv_evict("mem_k1", False))
            cut_phase(act, True, "mem_v1", kv_evict("mem_v1", True))
            act.wait_ge(fw_loaded, 16)
            act.activation(fwhi[:, :, :], fwraw[:, :, :], ACT.Copy).then_inc(fw_hi, 1)
            cut_phase(act, True, "in_qf", copy_evict(act, "in_qf", 0))
            cut_phase(act, True, "in_i", token_evict(act, "in_i", V_TOK))
            cut_phase(act, True, "in_gqk", copy_evict(act, "in_gqk", 24))
            act.wait_ge(stored, 32)
            cut_phase(act, True, "in_v", token_evict(act, "in_v", slot_tok(6, HG)))
            phase_over(act, "in_v")
            act.activation(T[0], rflat[:, 1, :], ACT.Sigmoid).then_inc(g_sig, 1)
            act.activation(GS, GS, ACT.Silu).then_inc(g_act, 1)
            act.wait_ge(g_seq, 2)
            act.activation(rflat[:, 1, :], T[0], ACT.Ln).then_inc(g_act, 1)
            act.wait_ge(g_seq, 10)
            act.activation(T[0], T[2], ACT.Exp).then_inc(g_act, 1)
            act.wait_ge(g_seq, 12)
            act.activation(T[0], T[2], ACT.Exp, scale=-1.0).then_inc(g_act, 1)
            act.wait_ge(g_seq, 14)
            act.activation(T[0], T[0], ACT.Exp).then_inc(g_act, 1)
            act.wait_ge(fg_seq, 3)
            act.activation(fgt[:, 1, :, :], fgt[:, 0, :, :], ACT.Exp, scale=-1.0).then_inc(fg_act, 1)
            act.wait_ge(fg_act, 1)
            act.activation(fgt[:, 1, :, :], fgt[:, 1, :, :], ACT.Ln, bias=one1[:, 0:1]).then_inc(fg_act, 1)
            for step in range(HH + 2):
                h = step
                if h < HH:
                    act.wait_ge(r_a, h + 1)
                    if h >= 2:
                        act.wait_ge(r_kv, h - 1)
                    act.activation(kend_sb[h % 2][0:CHUNK, 0:256], SB[0:CHUNK, h % 2, 256:512], ACT.Copy)
                    act.activation(kend_sb[h % 2][CHUNK:P, 256:384], SB[CHUNK:P, h % 2, 256:384], ACT.Copy)\
                        .then_inc(r_kt, 1)
                h = step - 2
                if 0 <= h < HH:
                    act.wait_ge(r_o, h + 1)
                    act.activation(head(OUT, h), OB[:, 0:256], ACT.Copy).then_inc(r_oev, 1)
            act.wait_ge(r_oev, HH)
            act.activation(T[2], OUT, ACT.Square).then_inc(r_sq, 1)
            for b in range(4):
                act.wait_ge(r_stat, b + 1)
                act.activation(T[1][:, b * 512:(b + 1) * 512], G[:, b, :], ACT.Ln, bias=epsr[:, 0:1],
                               scale=float(D // P)).then_inc(r_ln, 1)
            act.wait_ge(r_ln, 4)
            act.activation(T[1], T[1], ACT.Exp, scale=-0.5).then_inc(r_rstd, 1)
            act.wait_ge(r_seq, 2)
            act.activation(ah[:, 0:HH, :], ablk[:, 0:HH, :], ACT.Copy).then_inc(r_hi, 1)
            act_heads(act, fox)
            cut_phase(act, True, "out", no_evict)
            phase_over(act, "out")
            act_norm_squares(act, 1)
            act_norm_scale(act, 1)
            act_norm_out(act, 1)

            def ffn_evict(name):
                p = phases[name]
                b0 = int(name[-1]) * (HB // 2)

                def evict(i, cb):
                    n = i + b0
                    if cb == 0:
                        chunk_wait(act, p, i, 0)
                        act.wait_ge(conv_cur, n + 1)
                        for b in range(2):
                            act.activation(cbuf[:, b, :], G[:, b, 0:256], ACT.Identity, scale=convc[:, b, 2:3],
                                           bias=convc[:, b, 3:4]).then_inc(conv_c, 1)
                    else:
                        left_wait(act, p, i, 0)
                        act.activation(sbuf_[:, :, :], cbuf[:, :, :], ACT.Silu).then_inc(conv_s, 1)
                        left_wait(act, p, i, 1)
                        act.activation(hh[:, ds(i * 2, 2), :], hv[:, :, :], ACT.Copy).then_inc(h_hi, 1)
                return evict

            for half in range(2):
                cut_phase(act, True, f"ffn{half}", ffn_evict(f"ffn{half}"))
                cut_phase(act, True, f"down{half}", no_evict)
            phase_over(act, "down1")
            act_norm_squares(act, 2)
            act_norm_scale(act, 2)
            act_norm_out(act, 2)
            cut_phase(act, True, "in0_branch", copy_evict(act, "in0_branch", 0))

            def pool_hi(m):
                if m % 3 == 0:
                    g = m // 3
                    act.wait_ge(p_hi, 2 * g + 1)
                    act.activation(ph_[:, PG * g:PG * g + PG, :], pool_out(g), ACT.Copy).then_inc(p_hi, 1)

            cut_phase(act, True, "in0_gate", copy_evict(act, "in0_gate", 12), between=pool_hi)
            act.wait_ge(p_lo, 4)
            cut_phase(act, True, "in0", copy_evict(act, "in0", 24))
            phase_over(act, "in0")
            act.activation(ablk[:, 12:24, :], ablk[:, 12:24, :], ACT.Silu).then_inc(silu_done, 1)
            act.activation(ablk[:, 28:32, :], ablk[:, 28:32, :], ACT.Silu).then_inc(silu_done, 1)

            def pool_evict(i, cb):
                c = 2 * i + cb
                left_wait(act, phases["pool"], i, cb)
                act.activation(ah[:, 2 * c:2 * c + 2, :], blocks(sflat[:, 28 * TOK:30 * TOK]), ACT.Copy).then_inc(pm_h, 1)

            cut_phase(act, True, "pool", pool_evict)
            act_heads(act, heads_a)
            cut_phase(act, True, "out0", no_evict)
            act_norm_squares(act, 3)
            act_norm_scale(act, 3)
            act_norm_out(act, 3)
            cut_phase(act, True, "kvs_k", copy_evict(act, "kvs_k", 0))
            cut_phase(act, True, "kvs_v", token_evict(act, "kvs_v", vshared))
            cut_phase(act, True, "in1_q", copy_evict(act, "in1_q", 24))
            cut_phase(act, True, "in1_gate", copy_evict(act, "in1_gate", 36),
                      between=lambda m: act_heads(act, moba, m, m + 1))
            act_heads(act, moba, BB)
            act.wait_ge(s_o, 24)
            cut_phase(act, True, "in1", copy_evict(act, "in1", 48))
            phase_over(act, "in1")
            act.activation(ablk[:, 36:48, :], ablk[:, 36:48, :], ACT.Silu).then_inc(silu_done, 1)
            act.activation(ablk[:, 52:56, :], ablk[:, 52:56, :], ACT.Silu).then_inc(silu_done, 1)
            act_heads(act, heads_b)
            for q in range(4):
                act.wait_ge(b_val, q + 1)
                act.activation(ah[:, 3 * q:3 * q + 3, :], ablk[:, 24 + 3 * q:27 + 3 * q, :], ACT.Copy).then_inc(b_hi, 1)
            cut_phase(act, True, "out1", no_evict)
            act_norm_squares(act, 4)
            act_norm_scale(act, 4)
            act_norm_out(act, 4, split=False)
            for n in range(0, 8, 2):
                act.wait_ge(o_t, n + 1)
                if n:
                    act.wait_ge(o_sb, n)
                act.activation(sflat[:, n * 512:(n + 1) * 512], G[:, n % 4, :], ACT.Copy).then_inc(o_sb, 1)

        @block.vector
        def _(dve):
            counts = {}

            def link(sm, ins):
                key = sm.name
                counts[key] = counts.get(key, 0) + 1
                ins.then_inc(sm, 1)
                dve.wait_ge(sm, counts[key])

            dve.wait_ge(consts, 1)
            splits(dve, False, order[0], 0, 0)
            for g in range(8):
                dve.wait_ge(mem_hi, g + 1)
                dve.tensor_tensor(meml[:, 2 * g:2 * g + 2, :], blocks(XP[g % 4]),
                                  memh[:, 2 * g:2 * g + 2, :].bitcast(F32), ALU.subtract).then_inc(mem_lo, 1)
            dve.wait_ge(vec_t, 1)
            dve.tensor_copy(colv[:, 0:124], XP[0][:, 0:124])
            dve.tensor_copy(colv[:, 124:229], XP[0][:, P:P + 105])
            link(vec_ready, dve.tensor_copy(colv[:, 229:317], XP[0][:, 2 * P:2 * P + 88]))
            dve.tensor_copy(convp[:, :, 0:2], colv[:, 124:212].rearrange("p (j b) -> p b j", j=2))
            dve.tensor_copy(convp[:, :, 2:4], colv[:, 229:317].rearrange("p (j b) -> p b j", j=2))
            p0, p1 = colv[:, 212:220], colv[:, 220:228]
            link(lb_chain, dve.tensor_tensor(lbt[:, 2, :], p0, p1, ALU.max))
            dve.tensor_tensor(lbt[:, 0, :], p0, lbt[:, 2, :], ALU.subtract).then_inc(lb_chain, 1)
            dve.tensor_tensor(lbt[:, 1, :], p1, lbt[:, 2, :], ALU.subtract).then_inc(lb_chain, 1)
            counts[lb_chain.name] = 3
            cut_phase(dve, False, "mem_k0", no_evict)
            dve_norm(dve, 0)
            dve.wait_ge(lb_exp, 1)
            link(lb_chain, dve.tensor_tensor(lbt[:, 0, :], lbt[:, 2, :], lbt[:, 3, :], ALU.add))
            link(lb_chain, dve.reciprocal(lbt[:, 1, :], lbt[:, 0, :]))
            link(lb_chain, dve.tensor_tensor(lb[:, :], lbt[:, 2, :], lbt[:, 1, :], ALU.mult))
            link(lb_chain, dve.tensor_scalar(omlb[:, :], lb[:, :], -1.0, 1.0, ALU.mult, ALU.add))
            for n in ("mem_v0", "mem_k1", "mem_v1"):
                cut_phase(dve, False, n, no_evict)
            dve.wait_ge(fw_hi, 1)
            dve.tensor_tensor(fwlo[:, :, :], fwraw[:, :, :], fwhi[:, :, :].bitcast(F32), ALU.subtract).then_inc(fw_lo, 1)
            cut_phase(dve, False, "in_qf", no_evict)
            dve.wait_ge(fg_done, 1)
            dve.wait_ge(fb_loaded, 16)
            link(fg_seq, dve.tensor_tensor(fgate[:, :, :], TB[:, 0:2 * HH].rearrange("p (a b) -> p a b", a=2),
                                           fbias[:, :].unsqueeze(1).broadcast_to([P, TT, HH]), ALU.add))
            link(fg_seq, dve.tensor_scalar(fgt[:, 0, :, :], fgate[:, :, :], -1.0, None, ALU.mult))
            link(fg_seq, dve.tensor_tensor(fgt[:, 0, :, :], fgt[:, 0, :, :], fgate[:, :, :], ALU.max))
            for n in ("in_i", "in_gqk", "in_v"):
                cut_phase(dve, False, n, no_evict)
            dve.wait_ge(g_sig, 1)
            for h in range(HH):
                ins = dve.tensor_scalar(head(T[0], h), head(T[0], h), omlb[:, h:h + 1], lb[:, h:h + 1], ALU.mult, ALU.add)
            link(g_seq, ins)
            link(g_seq, dve.tensor_scalar(T[1], T[0], -1.0, 1.0, ALU.mult, ALU.add))
            dve.wait_ge(g_act, 2)
            for h in range(HH):
                dve.tensor_tensor_scan(head(T[2], h), scanmask[:, :], head(rflat[:, 1, :], h), 0.0,
                                       ALU.mult, ALU.add).then_inc(g_seq, 1)
            dve.wait_ge(g_act, 3)
            dve.tensor_copy(decay[:, :, :], T[0].rearrange("p (h n c) -> p h n c", h=HH, c=CHUNK)[:, :, :, CHUNK - 1])\
                .then_inc(g_seq, 1)
            dve.scalar_tensor_tensor(QD, QD, SCALE, T[0], ALU.mult, ALU.mult).then_inc(g_seq, 1)
            dve.wait_ge(g_act, 4)
            dve.tensor_tensor(KD, T[1], T[0], ALU.mult).then_inc(g_seq, 1)
            b4 = T[2].rearrange("p (n c) -> p n c", c=CHUNK)
            dve.wait_ge(g_seq, 13)
            dve.tensor_tensor(T[0].rearrange("p (n c) -> p n c", c=CHUNK),
                              b4[:, :, CHUNK - 1:CHUNK].broadcast_to([P, HH * NCH, CHUNK]), b4, ALU.subtract).then_inc(g_seq, 1)
            dve.wait_ge(g_act, 5)
            dve.tensor_tensor(KE, T[1], T[0], ALU.mult).then_inc(g_seq, 1)
            dve.wait_ge(g_seq, 15)
            dve.memset(T[0][:, 0:1280], 0.0).then_inc(r_attn, 1)
            dve.wait_ge(r_attn, 1)

            for step in range(HH + 1):
                h = step
                if h < HH:
                    dve.wait_ge(r_kt, h + 1)
                    if h >= 2:
                        dve.wait_ge(r_o, h - 1)
                    dve.copy_predicated(attn_sb[h % 2].rearrange("p (a b) -> p a b", a=2),
                                        chunktri[:, :].bitcast(U32).unsqueeze(1).broadcast_to([P, 2, P]),
                                        SB[:, h % 2, 0:256].rearrange("p (a b) -> p a b", a=2)).then_inc(r_attn, 1)
                h = step - 1
                if 0 <= h < HH:
                    dve.wait_ge(r_kv, h + 1)
                    if h >= 2:
                        dve.wait_ge(r_o, h - 1)
                    st = state[h % 2]
                    dve.tensor_copy(st[:, 0, :], TB[:, 0:P]).then_inc(r_state, 1)
                    for n in (1, 2):
                        dve.wait_ge(r_state, 3 * h + n)
                        dve.scalar_tensor_tensor(st[:, n, :], st[:, n - 1, :], decay[:, h, n:n + 1],
                                                 TB[:, n * P:(n + 1) * P], ALU.mult, ALU.add).then_inc(r_state, 1)
            dve.wait_ge(fg_act, 2)
            dve.wait_ge(r_oev, HH)
            link(fg_seq, dve.memset(ablk[:, 10, :], 0.0))
            link(fg_seq, dve.tensor_scalar(fgate[:, :, :], fgate[:, :, :], 0.0, None, ALU.min))
            link(fg_seq, dve.tensor_tensor(fgt[:, 0, :, :], fgate[:, :, :], fgt[:, 1, :, :], ALU.subtract))
            link(fg_seq, dve.tensor_copy(flf[:, :, 0:HH], fgt[:, 0, :, :]))
            dve.wait_ge(r_rstd, 1)
            link(r_seq, dve.scalar_tensor_tensor(OUT, OUT, colv[:, 228:229], T[1], ALU.mult, ALU.mult))
            link(r_seq, dve.tensor_tensor(OUT, OUT, GS, ALU.mult))
            dve.wait_ge(r_hi, 1)
            dve.tensor_tensor(al[:, 0:HH, :], ablk[:, 0:HH, :], ah[:, 0:HH, :].bitcast(F32), ALU.subtract).then_inc(r_hi, 1)
            dve.wait_ge(fc_done, 1)
            dve.tensor_copy(fcT[:, 0:P], TB[:, 0:P])
            dve.wait_ge(fc_done, 2)
            link(fc_ready, dve.tensor_scalar(fcT[:, P:TOK], TB[:, P:TOK], float(D), None, ALU.mult))
            link(fc_ready, dve.tensor_tensor(fcT[:, P:TOK], fcT[:, P:TOK], OB[:, 0:P], ALU.add))
            link(fc_ready, dve.tensor_scalar(fcN, fcT, -1.0, None, ALU.mult))
            dve.wait_ge(r_hi, 2)
            dve.tensor_scalar(rflat[:, 4, :], rflat[:, 4, :], SCALE, None, ALU.mult).then_inc(fc_ready, 1)
            dve_heads(dve, fox)
            cut_phase(dve, False, "out", residual_evict(dve, "out"))
            dve_norm(dve, 1)

            def ffn_evict(name):
                p = phases[name]
                b0 = int(name[-1]) * (HB // 2)

                def evict(i, cb):
                    n = i + b0
                    if cb == 0:
                        dve.tensor_copy(convc[:, :, :], convp[:, ds(i * 2 + 2 * b0, 2), :]).then_inc(conv_cur, 1)
                        dve.wait_ge(conv_cur, n + 1)
                        for b in range(2):
                            dve.wait_ge(conv_c, n * 2 + (b + 1))
                            dve.scalar_tensor_tensor(cbuf[:, b, 1:TOK], G[:, b, 0:TOK - 1], convc[:, b, 1:2],
                                                     cbuf[:, b, 1:TOK], ALU.mult, ALU.add).then_inc(conv_1, 1)
                        for b in range(2):
                            dve.wait_ge(conv_1, n * 2 + (b + 1))
                            ins = dve.scalar_tensor_tensor(cbuf[:, b, 2:TOK], G[:, b, 0:TOK - 2], convc[:, b, 0:1],
                                                           cbuf[:, b, 2:TOK], ALU.mult, ALU.add)
                        ins.then_inc(pair_free[0], 1)
                    else:
                        chunk_wait(dve, p, i, 1)
                        dve.wait_ge(conv_s, n + 1)
                        ins = dve.tensor_tensor(hv[:, :, :], sbuf_[:, :, :], G[:, 2:4, 0:256], ALU.mult)
                        ins.then_inc(pair_free[1], 1)
                        dve.wait_ge(h_hi, n + 1)
                        dve.tensor_tensor(hl[:, ds(i * 2, 2), :], hv[:, :, :], hh[:, ds(i * 2, 2), :].bitcast(F32),
                                          ALU.subtract).then_inc(h_lo, 1)
                return evict

            for half in range(2):
                cut_phase(dve, False, f"ffn{half}", ffn_evict(f"ffn{half}"))
                cut_phase(dve, False, f"down{half}", residual_evict(dve, f"down{half}"))
            dve_norm(dve, 2)
            cut_phase(dve, False, "in0_branch", no_evict)
            phase_over(dve, "in0_branch")
            link(p_seq, dve.memset(flat[:, 24 * TOK:24 * TOK + 2 * PG * W], 0.0))

            def pool_group(m):
                if m % 3:
                    return
                g = m // 3
                w, src = WINDOWS[g], ablk[:, PG * g:PG * g + PG, :]
                link(p_seq, dve.tensor_copy(pads[0][:, :, PAD:W], src))
                cur, k = 0, 1
                while k < w:
                    link(p_seq, dve.tensor_tensor(pads[1 - cur][:, :, PAD:W], pads[cur][:, :, PAD:W],
                                                  pads[cur][:, :, PAD - k:W - k], ALU.add))
                    cur, k = 1 - cur, 2 * k
                pm = pool_out(g)
                link(p_seq, dve.tensor_scalar(pm, pads[cur][:, :, PAD:W], 1.0 / w, None, ALU.mult))
                link(p_seq, dve.tensor_tensor(pm[:, :, 0:w - 1], pads[cur][:, :, PAD:PAD + w - 1],
                                              invcnt[:, 0:w - 1].unsqueeze(1).broadcast_to([P, PG, w - 1]), ALU.mult))
                dve.tensor_tensor(pm, pm, src, ALU.subtract).then_inc(p_hi, 1)
                dve.wait_ge(p_hi, 2 * g + 2)
                dve.tensor_tensor(pl_[:, PG * g:PG * g + PG, :], pm, ph_[:, PG * g:PG * g + PG, :].bitcast(F32),
                                  ALU.subtract).then_inc(p_lo, 1)
                dve.wait_ge(p_lo, g + 1)

            cut_phase(dve, False, "in0_gate", no_evict, between=pool_group)
            cut_phase(dve, False, "in0", no_evict)
            phase_over(dve, "in0")
            dve.wait_ge(silu_done, 2)
            pmix = blocks(sflat[:, 28 * TOK:30 * TOK])

            def pool_evict(i, cb):
                c = 2 * i + cb
                chunk_wait(dve, phases["pool"], i, cb)
                if c:
                    dve.wait_ge(pm_l, c)
                for b in range(2):
                    j = 2 * c + b
                    ins = dve.scalar_tensor_tensor(pmix[:, b, :], G[:, 2 * cb + b, 0:256], colv[:, 112 + j:113 + j],
                                                   ablk[:, 12 + j, :], ALU.mult, ALU.mult)
                ins.then_inc(pair_free[cb], 1)
                dve.wait_ge(pm_h, c + 1)
                dve.tensor_tensor(al[:, 2 * c:2 * c + 2, :], pmix, ah[:, 2 * c:2 * c + 2, :].bitcast(F32),
                                  ALU.subtract).then_inc(pm_l, 1)

            cut_phase(dve, False, "pool", pool_evict)
            dve.tensor_scalar(ablk[:, 24:28, :], ablk[:, 24:28, :], SCALE, None, ALU.mult).then_inc(q_scaled, 1)
            dve_heads(dve, heads_a)
            cut_phase(dve, False, "out0", residual_evict(dve, "out0", ALPHA))
            dve_norm(dve, 3)
            for n in ("kvs_k", "kvs_v", "in1_q"):
                cut_phase(dve, False, n, no_evict)
            phase_over(dve, "in1_q")
            dve.tensor_scalar(ablk[:, 24:36, :], ablk[:, 24:36, :], SCALE, None, ALU.mult).then_inc(q_scaled, 1)
            cut_phase(dve, False, "in1_gate", no_evict, between=lambda m: dve_heads(dve, moba, m, m + 1))
            dve_heads(dve, moba, BB)
            cut_phase(dve, False, "in1", no_evict)
            phase_over(dve, "in1")
            dve.tensor_scalar(ablk[:, 48:52, :], ablk[:, 48:52, :], SCALE, None, ALU.mult).then_inc(q_scaled, 1)
            dve.wait_ge(silu_done, 4)
            dve.wait_ge(s_tmp, 24)
            for q in range(4):
                o = ablk[:, 24 + 3 * q:27 + 3 * q, :]
                dve.tensor_tensor(o, o, ablk[:, 36 + 3 * q:39 + 3 * q, :], ALU.mult).then_inc(b_val, 1)
            dve_heads(dve, heads_b)
            for q in range(4):
                dve.wait_ge(b_hi, q + 1)
                dve.tensor_tensor(al[:, 3 * q:3 * q + 3, :], ablk[:, 24 + 3 * q:27 + 3 * q, :],
                                  ah[:, 3 * q:3 * q + 3, :].bitcast(F32), ALU.subtract).then_inc(b_lo, 1)
            cut_phase(dve, False, "out1", residual_evict(dve, "out1", ALPHA))
            dve_norm(dve, 4, split=False)
            for n in range(1, 8, 2):
                dve.wait_ge(o_t, n + 1)
                dve.wait_ge(o_sb, n)
                dve.tensor_copy(sflat[:, n * 512:(n + 1) * 512], G[:, n % 4, :]).then_inc(o_sb, 1)


_INS = {"x": "x", "norm1": "norm1_gain", "w_in": "w_in", "lbp": "hgrn_lb_param", "hgain": "hgrn_norm_gain",
        "fox_bias": "fox_gate_bias", "w_out": "w_out", "norm2": "norm2_gain", "w_ffn_gate": "w_ffn_gate",
        "w_ffn_up": "w_ffn_up", "conv_w": "ffn_conv_w", "conv_b": "ffn_conv_b", "w_ffn_down": "w_ffn_down",
        "final": "final_norm_gain", "mem": "mem_2", "w_in_2": "w_in_2", "w_out_2": "w_out_2",
        "w_mem_kv": "w_mem_kv_2", "ln_g": "ln_g_2", "ln_b": "ln_b_2", "pool_w": "pool_w_2",
        "pool_scale": "pool_scale_2", "w_kv": "w_kv_shared_2"}
_FIRST = ("x", "mem", "w_in", "w_out", "w_ffn_gate", "w_ffn_up", "conv_w", "w_ffn_down", "pool_w")


def kernel(**inputs):
    import numpy as np
    import concourse.bacc as bacc
    from concourse.bass_utils import run_bass_kernel_spmd

    nc = bacc.Bacc("TRN2", target_bir_lowering=False, num_devices=1)
    arrays, aps = {}, {}
    for key, name in _INS.items():
        a = np.ascontiguousarray(inputs[name])
        arrays[f"in_{name}"] = a
        ap = nc.dram_tensor(f"in_{name}", a.shape, mybir.dt.from_np(a.dtype), kind="ExternalInput").ap()
        aps[key] = ap[0] if key in _FIRST else ap.unsqueeze(0) if key == "final" else ap
    result = nc.dram_tensor("result", (1, TOK, D), F32, kind="ExternalOutput").ap()
    aps["result"] = result[0]
    program(nc, aps)
    r = run_bass_kernel_spmd(nc, [arrays], core_ids=[0])
    return r.results[0]["result"]
```

```python
import concourse.bass as bass
from concourse import mybir
from contextlib import ExitStack

F32 = mybir.dt.float32
F32R = mybir.dt.float32r
U32 = mybir.dt.uint32
ALU = mybir.AluOpType
ACT = mybir.ActivationFunctionType
AX = mybir.AxisListType

P = 128
TOK = 256
TT = TOK // P
D = 2048
KT = D // P
HG = 1024
HH = HG // P
CHUNK = 64
NCH = TOK // CHUNK
DFF = 5632
FB = DFF // P
HB = FB // 2
BR = 1536
BB = BR // P
MH = 4
PG = 3
WINDOWS = (2, 4, 8, 16)
PAD = 16
EPS = 1e-6
LN_EPS = 1e-5
ALPHA = (2 * 2) ** 0.25
SCALE = float(P) ** -0.5
NEG = -1e30
SLOT = 2048
ds = bass.ds


class Phase:

    def __init__(self, name, bodies, tpc, size, source, mats, form, rhs, first):
        self.name, self.bodies, self.tpc, self.size = name, bodies, tpc, size
        self.source, self.mats, self.form, self.rhs = source, mats, form, rhs
        self.tile0, self.chunk0 = first
        self.tpb = 2 * tpc
        self.end = (self.tile0 + bodies * self.tpb, self.chunk0 + bodies * 2)


def program(nc, A):
    ctx = ExitStack()
    with ctx:
        def sb(name, shape, dt=F32):
            return ctx.enter_context(nc.sbuf_tensor(name, shape, dt))

        def sem(name):
            return ctx.enter_context(nc.semaphore(name))

        ident = sb("ident", [P, P])
        meanw = sb("meanw", [P, P])
        maskneg = sb("maskneg", [P, P])
        tri01 = sb("tri01", [P, P])
        chunktri = sb("chunktri", [P, P])
        scanmask = sb("scanmask", [P, TOK])
        colv = sb("colv", [P, 321])
        convp = sb("convp", [P, FB, 4])
        convc = sb("convc", [P, 2, 4])
        epsr = sb("epsr", [P, 1])
        epsl = sb("epsl", [P, 1])
        one1 = sb("one1", [P, 1])
        invcnt = sb("invcnt", [P, PAD])
        lb = sb("lb", [P, HH])
        omlb = sb("omlb", [P, HH])
        lbt = sb("lbt", [P, 4, HH])
        decay = sb("decay", [P, HH, NCH])
        rstd = sb("rstd", [P, TOK])
        nmax = sb("nmax", [P, 2, TT])
        psumr = sb("psumr", [P, 2, TT])
        pinv = sb("pinv", [P, 2, TT])
        fbias = sb("fbias", [P, 1])
        fwraw = sb("fwraw", [P, KT, HH])

        base = (nc.sbuf_base + 31) // 32 * 32
        ctx.enter_context(nc.sbuf_tensor("fence", [P, 200 * 256], F32))
        K = 1024

        def at(name, kib, shape, dt=F32):
            return nc.alloc_sbuf_tensor_at(name, shape, dt, offset=base + int(kib * K))

        raw = at("raw", 0, [P, 4, SLOT])
        hi = at("hi", 32, [P, 4, SLOT], F32R)
        lo = at("lo", 64, [P, 4, SLOT], F32R)
        xres = at("xres", 96, [P, KT, TOK])
        ah = at("ah", 112, [P, KT, TOK], F32R)
        al = at("al", 128, [P, KT, TOK], F32R)
        scr = at("scr", 112, [P, 4, SLOT])
        arena = at("arena", 144, [P, 7, SLOT])
        memtok = at("memtok", 112, [P, TT, D])
        xtok = at("xtok", 128, [P, TT, D])
        memh = at("memh", 144, [P, KT, TOK], F32R)
        meml = at("meml", 160, [P, KT, TOK], F32R)
        normt = at("normt", 176, [P, KT, TOK])
        vrows = at("vrows", 184, [P, 3, P])
        stage = at("stage", 192, [P, SLOT])
        fwhi = at("fwhi", 176, [P, KT, P], F32R)
        fwlo = at("fwlo", 184, [P, KT, P], F32R)
        ringscr = at("ringscr", 48, [P, 2 * SLOT])
        hh = at("hh", 144, [P, HB, TOK], F32R)
        hl = at("hl", 144 + HB, [P, HB, TOK], F32R)
        cbuf = at("cbuf", 188, [P, 2, TOK])
        sbuf_ = at("silub", 190, [P, 2, TOK])
        hv = at("hv", 192, [P, 2, TOK])
        ph_ = at("pooledh", 176, [P, BB, TOK], F32R)
        pl_ = at("pooledl", 188, [P, BB, TOK], F32R)

        def blocks(t, n=8):
            return t.rearrange("p (b t) -> p b t", t=TOK)

        flat = arena[:, :, :].rearrange("p s n -> p (s n)")
        ablk = flat.rearrange("p (b t) -> p b t", t=TOK)
        sflat = scr[:, :, :].rearrange("p s n -> p (s n)")
        sblk = sflat.rearrange("p (b t) -> p b t", t=TOK)
        rflat = arena[:, :, :]

        G = ctx.enter_context(nc.psum_tensor("G", [P, 4, 512], F32))
        SB = ctx.enter_context(nc.psum_tensor("SB", [P, 2, 512], F32))
        TB = ctx.enter_context(nc.psum_tensor("TB", [P, 512], F32))
        OB = ctx.enter_context(nc.psum_tensor("OB", [P, 512], F32))
        XP = [SB[:, 0, :], SB[:, 1, :], TB[:, :], OB[:, :]]

        memkv = nc.dram_tensor("memkv_scratch", (2, P, SLOT), F32, kind="Internal").ap()

        raw_loaded = [sem(f"raw_loaded{s}") for s in range(4)]
        hi_ready, lo_ready, tile_used = sem("hi_ready"), sem("lo_ready"), sem("tile_used")
        pair_free = [sem("pair_free0"), sem("pair_free1")]
        consts = sem("consts")
        pool_seq = sem("pool_seq")
        vec_loaded, mem_loaded, x_loaded = sem("vec_loaded"), sem("mem_loaded"), sem("x_loaded")
        vec_t, vec_ready = sem("vec_t"), sem("vec_ready")
        in_t, mem_hi, mem_lo, x_ready = sem("in_t"), sem("mem_hi"), sem("mem_lo"), sem("x_ready")
        lb_chain = sem("lb_chain")
        lb_exp = sem("lb_exp")
        stored, reloaded, out_stored = sem("stored"), sem("reloaded"), sem("out_stored")
        n_mean, n_xc, n_sq, n_stat = sem("n_mean"), sem("n_xc"), sem("n_sq"), sem("n_stat")
        n_ln, n_rstd, n_y, n_b, n_hi, n_lo = (sem("n_ln"), sem("n_rstd"), sem("n_y"), sem("n_b"),
                                              sem("n_hi"), sem("n_lo"))
        fw_loaded, fb_loaded, fw_hi, fw_lo = sem("fw_loaded"), sem("fb_loaded"), sem("fw_hi"), sem("fw_lo")
        fg_done, fg_seq, fg_act, fw_zero = sem("fg_done"), sem("fg_seq"), sem("fg_act"), sem("fw_zero")
        f_hi, f_lo = sem("f_hi"), sem("f_lo")
        g_sig, g_seq, g_ln, g_act = sem("g_sig"), sem("g_seq"), sem("g_ln"), sem("g_act")
        r_a, r_kt, r_attn, r_kv, r_state, r_o, r_oev = (sem("r_a"), sem("r_kt"), sem("r_attn"),
                                                       sem("r_kv"), sem("r_state"), sem("r_o"), sem("r_oev"))
        r_sq, r_stat, r_ln, r_rstd, r_seq, r_hi, r_lo = (sem("r_sq"), sem("r_stat"), sem("r_ln"), sem("r_rstd"),
                                                  sem("r_seq"), sem("r_hi"), sem("r_lo"))
        conv_cur, conv_c, conv_1, conv_s, h_hi, h_lo = (
            sem("conv_cur"), sem("conv_c"), sem("conv_1"), sem("conv_s"), sem("h_hi"), sem("h_lo"))
        s_sc, s_mx, s_exp, s_inv, s_p, s_t, s_tc, s_o, s_tmp, s_hi, s_lo = (
            sem("s_scores"), sem("s_max"), sem("s_exp"), sem("s_inv"), sem("s_probs"), sem("s_probsT"),
            sem("s_probsT_sb"), sem("s_out"), sem("s_out_sb"), sem("s_out_hi"), sem("s_out_lo"))
        silu_done, p_seq, p_hi, p_lo = sem("silu_done"), sem("p_seq"), sem("p_hi"), sem("p_lo")
        pm_h, pm_l = sem("pm_hi"), sem("pm_lo")
        o_t, o_sb = sem("o_t"), sem("o_sb")
        q_scaled = sem("q_scaled")
        a_val, a_hi, a_lo = sem("a_value"), sem("a_hi"), sem("a_lo")
        n_sumx, n_sums = sem("n_sumx"), sem("n_sums")
        b_val, b_hi, b_lo = sem("b_value"), sem("b_hi"), sem("b_lo")

        def kview(w):
            return w.rearrange("(t p) n -> p t n", p=P)

        def std(w, col, cols_of_body=512):
            v = kview(w)

            def source(i, j):
                return v[:, (j % 2) * 8:(j % 2) * 8 + 8, ds(i * cols_of_body + (col + (j // 2) * 256), 256)]
            return source

        def ffn_source(half):
            vg, vu = kview(A["w_ffn_gate"]), kview(A["w_ffn_up"])

            def source(i, j):
                v = vg if j < 2 else vu
                return v[:, (j % 2) * 8:(j % 2) * 8 + 8, ds(i * 256 + half * HB * P, 256)]
            return source

        def down_source(half):
            v = kview(A["w_ffn_down"])

            def source(i, j):
                t = half * HB + (j % 2) * (HB // 2)
                return v[:, t:t + HB // 2, ds(i * 512 + (j // 2) * P, P)]
            return source

        def pool_source(i, j):
            b = i * 4 + j
            return A["pool_w"][b // PG].rearrange("(t p) n -> p t n", p=P)[:, :, (b % PG) * P:(b % PG + 1) * P]

        def std_mats(i, j):
            return [(b, [(k, (j % 2) * 8 + k) for k in range(8)], 256, b * P, j % 2 == 0, j % 2 == 1) for b in (0, 1)]

        def down_mats(i, j):
            n = HB // 2
            return [((j // 2) % 2, [(k, (j % 2) * n + k) for k in range(n)], P, 0, j % 2 == 0, j % 2 == 1)]

        def pool_mats(i, j):
            b = i * 4 + j
            return [(j % 2, [(k, b // PG * PG + k) for k in range(PG)], P, 0, True, True)]

        phases = {}
        at_ = [(0, 0)]

        def add(name, bodies, source, rhs, form="A", tpc=2, size=SLOT, mats=std_mats):
            p = phases[name] = Phase(name, bodies, tpc, size, source, mats, form, rhs, at_[0])
            at_[0] = p.end

        mem_ops, act_ops, h_ops, pool_ops = (memh, meml), (ah, al), (hh, hl), (ph_, pl_)
        for l in range(2):
            add(f"mem_k{l}", 1, std(A["w_mem_kv"][l], 0), mem_ops)
            add(f"mem_v{l}", 1, std(A["w_mem_kv"][l], 512), mem_ops, form="B")
        add("in_qf", 4, std(A["w_in"], 0), act_ops)
        add("in_i", 2, std(A["w_in"], 2 * HG), act_ops, form="B")
        add("in_gqk", 6, std(A["w_in"], 3 * HG), act_ops)
        add("in_v", 2, std(A["w_in"], 6 * HG), act_ops, form="B")
        add("out", 4, std(A["w_out"], 0), act_ops)
        for half in range(2):
            add(f"ffn{half}", HB // 2, ffn_source(half), act_ops)
            add(f"down{half}", 4, down_source(half), h_ops, tpc=4, size=HB // 2 * P, mats=down_mats)
        add("in0_branch", 3, std(A["w_in_2"][0], 0), act_ops)
        add("in0_gate", 3, std(A["w_in_2"][0], BR), act_ops)
        add("in0", 2, std(A["w_in_2"][0], 2 * BR), act_ops)
        add("pool", 3, pool_source, pool_ops, size=PG * P, mats=pool_mats)
        add("out0", 4, std(A["w_out_2"][0], 0), act_ops)
        add("kvs_k", 3, std(A["w_kv"], 0), act_ops)
        add("kvs_v", 3, std(A["w_kv"], BR), act_ops, form="B")
        add("in1_q", 3, std(A["w_in_2"][1], 0), act_ops)
        add("in1_gate", 3, std(A["w_in_2"][1], BR), act_ops)
        add("in1", 2, std(A["w_in_2"][1], 2 * BR), act_ops)
        add("out1", 4, std(A["w_out_2"][1], 0), act_ops)
        order = list(phases.values())
        follow = {p.name: q for p, q in zip(order, order[1:])}

        def tile_wait(eng, sm, value):
            if not isinstance(value, int) or value > 0:
                eng.wait_ge(sm, value)

        def sized(t, s, size):
            return t[:, s, 0:size]

        def sp_phase(eng, name):
            p = phases[name]

            def body(i):
                for j in range(p.tpb):
                    n = i * p.tpb + (p.tile0 + j)
                    tile_wait(eng, lo_ready, n - 3)
                    src = p.source(i, j)
                    dst = sized(raw, j % 4, p.size).rearrange("p (t n) -> p t n", t=src.shape[1])
                    eng.dma_start(dst, src).then_inc(raw_loaded[j % 4], 16)
            loop(eng, p.bodies, body, p.name == "pool")

        def loop(eng, n, body, unroll=False):
            if n == 1 or unroll:
                for i in range(n):
                    body(i)
            else:
                with eng.Fori(0, n) as i:
                    body(i)

        def splits(eng, act, p, i, first, count=None):
            for j in range(first, first + (count or p.tpc)):
                s = j % 4
                n = i * p.tpb + (p.tile0 + j)
                if act:
                    eng.wait_ge(raw_loaded[s], (i * p.tpb + (p.tile0 + j - s)) * 4 + 16)
                    tile_wait(eng, tile_used, n - 3)
                    eng.activation(sized(hi, s, p.size), sized(raw, s, p.size), ACT.Copy).then_inc(hi_ready, 1)
                else:
                    eng.wait_ge(hi_ready, n + 1)
                    eng.tensor_tensor(sized(lo, s, p.size), sized(raw, s, p.size),
                                      sized(hi, s, p.size).bitcast(F32), ALU.subtract).then_inc(lo_ready, 1)

        def cut_phase(eng, act, name, evict, between=None):
            p = phases[name]

            def body(i, nxt, ni):
                if between is not None:
                    splits(eng, act, p, i, 2, 1)
                    between(4 * i)
                    splits(eng, act, p, i, 3, 1)
                    between(4 * i + 1)
                    evict(i, 0)
                    splits(eng, act, nxt, ni, 0, 1)
                    between(4 * i + 2)
                    splits(eng, act, nxt, ni, 1, 1)
                    between(4 * i + 3)
                    evict(i, 1)
                    return
                splits(eng, act, p, i, p.tpc)
                evict(i, 0)
                if nxt is not None:
                    splits(eng, act, nxt, ni, 0)
                evict(i, 1)
            if p.bodies > 1:
                loop(eng, p.bodies - 1, lambda i: body(i, p, i + 1), p.name == "pool" or between is not None)
            body(p.bodies - 1, follow.get(name), 0)

        def no_evict(i, cb):
            pass

        def pe_phase(eng, name, between=None, norm=None, halves=None):
            p = phases[name]
            xh, xl = p.rhs

            def body(i):
                for j in range(p.tpb):
                    s, cb = j % 4, j // p.tpc
                    eng.wait_ge(lo_ready, i * p.tpb + (p.tile0 + j + 1))
                    if norm is not None:
                        eng.wait_ge(n_lo, 4 * norm + 2 + 2 * (j % 2))
                    if halves is not None:
                        for ready, count in halves[j % 2]:
                            eng.wait_ge(ready, count)
                    if j % p.tpc == 0:
                        tile_wait(eng, pair_free[cb], i + p.chunk0 // 2)
                    if name.startswith("down") and j < 2:
                        half = int(name[-1])
                        eng.wait_ge(h_lo, HB // 2 * half + (6 if j == 0 else 11))
                    last = None
                    for b, ks, width, col, first, final in p.mats(i, j):
                        bank = 2 * cb + b
                        for q, (kt, k) in enumerate(ks):
                            st, sp = first and q == 0, final and q == len(ks) - 1
                            if p.form == "A":
                                w = slice(kt * width + col, kt * width + col + P)
                                wh, wl = hi[:, s, w], lo[:, s, w]
                                pairs = [(wh, xh[:, k, :]), (wh, xl[:, k, :]), (wl, xh[:, k, :])]
                            else:
                                w = slice(kt * width, (kt + 1) * width)
                                wh, wl = hi[:, s, w], lo[:, s, w]
                                t = slice(b * P, (b + 1) * P)
                                pairs = [(xh[:, k, t], wh), (xh[:, k, t], wl), (xl[:, k, t], wh)]
                            for r, (l_, r_) in enumerate(pairs):
                                last = eng.matmul(G[:, bank, 0:256], l_, r_, start=st and r == 0, stop=sp and r == 2)
                    last.then_inc(tile_used, 1)
                    if between is not None:
                        between(4 * i + j)
            loop(eng, p.bodies, body, p.name == "pool" or between is not None)

        def chunk_wait(eng, p, i, cb):
            eng.wait_ge(tile_used, i * p.tpb + (p.tile0 + (cb + 1) * p.tpc))

        def left_wait(eng, p, i, cb):
            eng.wait_ge(pair_free[cb], i + (p.chunk0 // 2 + 1))

        def copy_evict(eng, name, block0):
            p = phases[name]

            def evict(i, cb):
                chunk_wait(eng, p, i, cb)
                eng.activation(ablk[:, ds(i * 4 + (block0 + 2 * cb), 2), :], G[:, 2 * cb:2 * cb + 2, 0:256],
                               ACT.Copy).then_inc(pair_free[cb], 1)
            return evict

        def token_evict(eng, name, dst):
            p = phases[name]

            def evict(i, cb):
                chunk_wait(eng, p, i, cb)
                eng.activation(dst[:, :, ds(i * 512 + cb * 256, 256)], G[:, 2 * cb:2 * cb + 2, 0:256],
                               ACT.Copy).then_inc(pair_free[cb], 1)
            return evict

        def residual_evict(eng, name, alpha=None, norm=None):
            p = phases[name]

            def evict(i, cb):
                chunk_wait(eng, p, i, cb)
                x = xres[:, ds(i * 4 + 2 * cb, 2), :]
                g = G[:, 2 * cb:2 * cb + 2, 0:256]
                if alpha is None:
                    ins = eng.tensor_tensor(x, x, g, ALU.add)
                else:
                    ins = eng.scalar_tensor_tensor(x, x, alpha, g, ALU.mult, ALU.add)
                ins.then_inc(pair_free[cb], 1)
                if cb and norm is not None:
                    left_wait(eng, p, i, 0)
                    left_wait(eng, p, i, 1)
                    if norm >= 3:
                        sum_quarter(eng, xres[:, ds(i * 4, 4), :], i, n_sumx)
                    else:
                        eng.wait_ge(n_sq, i + (4 * norm + 1))
                        sum_quarter(eng, SQUARES[norm][:, ds(i * 4, 4), :], i, n_sums)
            return evict

        def phase_over(eng, name):
            n = phases[name].end[1] // 2
            eng.wait_ge(pair_free[0], n)
            eng.wait_ge(pair_free[1], n)

        NORMS = {0: (0, None, normt), 1: (16, None, normt), 2: (32, None, xres), 3: (48, 80, xres), 4: (64, 96, xres)}

        SQUARES = {0: normt, 1: normt, 2: sblk, 3: normt, 4: normt}
        part = ablk[:, 52:56, :]

        def sum_quarter(eng, src, q, sm):
            eng.tensor_reduce(part[:, q, :] if isinstance(q, int) else part[:, ds(q, 1), :].rearrange("p a t -> p (a t)"),
                              src.rearrange("p k t -> p t k"), AX.X, ALU.add).then_inc(sm, 1)

        def quarter(t, q):
            return t[:, 4 * q:4 * q + 4, :]

        def pe_norm(eng, u):
            if u >= 3:
                for q in range(4):
                    eng.wait_ge(n_sumx, 4 * (u - 3) + q + 1)
                    last = eng.matmul(OB[:, 0:TOK], meanw[:, :], part[:, q, :], start=q == 0, stop=q == 3)
                last.then_inc(n_mean, 1)
            if u in (1, 2):
                for q in range(4):
                    eng.wait_ge(n_sums, 4 * (u - 1) + q + 1)
                    last = eng.matmul(TB[:, 0:TOK], meanw[:, :], part[:, q, :], start=q == 0, stop=q == 3)
                last.then_inc(n_stat, 1)
                return
            for k in range(KT):
                if k % 4 == 0:
                    eng.wait_ge(n_sq, 4 * u + k // 4 + 1)
                last = eng.matmul(TB[:, 0:TOK], meanw[:, :], normt[:, k, :], start=k == 0, stop=k == KT - 1)
            last.then_inc(n_stat, 1)

        def act_norm_squares(eng, u):
            for q in range(4):
                if u >= 3:
                    eng.wait_ge(n_xc, 4 * (u - 3) + q + 1)
                eng.activation(quarter(normt, q), quarter(xres, q), ACT.Square).then_inc(n_sq, 1)

        def squares_evict(eng, name, u):
            p = phases[name]

            def evict(i, cb):
                if cb:
                    left_wait(eng, p, i, 0)
                    left_wait(eng, p, i, 1)
                    eng.activation(SQUARES[u][:, ds(i * 4, 4), :], xres[:, ds(i * 4, 4), :], ACT.Square).then_inc(n_sq, 1)
            return evict

        def act_norm_scale(eng, u):
            eng.wait_ge(n_stat, u + 1)
            eng.activation(rstd[:, :], TB[:, 0:TOK], ACT.Ln, bias=(epsl if u >= 3 else epsr)[:, 0:1]).then_inc(n_ln, 1)
            eng.wait_ge(n_ln, u + 1)
            eng.activation(rstd[:, :], rstd[:, :], ACT.Exp, scale=-0.5).then_inc(n_rstd, 1)

        def act_norm_out(eng, u, split=True, quarters=(0, 4)):
            gain, bias, dst = NORMS[u]
            for q in range(*quarters):
                if bias is None:
                    eng.wait_ge(n_y, 4 * u + q + 1)
                else:
                    eng.wait_ge(n_b, 4 * (u - 3) + q + 1)
                if split:
                    eng.activation(quarter(ah, q), quarter(dst, q), ACT.Copy).then_inc(n_hi, 1)

        def pool_norm_bias(eng, u):
            gain, bias, dst = NORMS[u]
            for q in range(4):
                eng.wait_ge(n_y, 4 * u + q + 1)
                eng.tensor_tensor(quarter(dst, q), quarter(dst, q),
                                  colv[:, bias + 4 * q:bias + 4 * q + 4].unsqueeze(2).broadcast_to([P, 4, TOK]),
                                  ALU.add).then_inc(n_b, 1)

        def dve_norm(eng, u, split=True, quarters=(0, 5)):
            gain, bias, dst = NORMS[u]
            if u >= 3:
                eng.wait_ge(n_mean, u - 2)
                for q in range(4):
                    eng.tensor_tensor(quarter(xres, q), quarter(xres, q),
                                      OB[:, 0:TOK].unsqueeze(1).broadcast_to([P, 4, TOK]), ALU.subtract).then_inc(n_xc, 1)
                eng.wait_ge(n_xc, 4 * (u - 2))
            eng.wait_ge(n_rstd, u + 1)
            for q in range(*quarters):
                if q < 4:
                    for k in range(4 * q, 4 * q + 4):
                        ins = eng.scalar_tensor_tensor(dst[:, k, :], xres[:, k, :], colv[:, gain + k:gain + k + 1],
                                                       rstd[:, :], ALU.mult, ALU.mult)
                    ins.then_inc(n_y, 1)
                if split and q > 0:
                    eng.wait_ge(n_hi, 4 * u + q)
                    eng.tensor_tensor(quarter(al, q - 1), quarter(dst, q - 1), quarter(ah, q - 1).bitcast(F32),
                                      ALU.subtract).then_inc(n_lo, 1)

        class Heads:

            def __init__(self, first, n, q, k, v, causal, out0, probs, gate=None, forget=False, cut=0):
                self.cut = cut
                self.first, self.n, self.q, self.k, self.v = first, n, q, k, v
                self.causal, self.out0, self.gate, self.forget = causal, out0, gate, forget
                if isinstance(probs, tuple):
                    probs, probst = probs
                else:
                    probs, probst = probs[:, 0:1024], probs[:, 1024:2048]
                self.p = [probs[:, 0:512].rearrange("p (a b) -> p a b", a=2),
                          probs[:, 512:1024].rearrange("p (a b) -> p a b", a=2)]
                self.t = [probst[:, 0:512], probst[:, 512:1024]]

        rblk = ringscr[:, :].rearrange("p (b t) -> p b t", t=TOK)
        fcT, fcN, fx, fe, ones = (rblk[:, 8 + b, :] for b in range(5))

        def pe_heads(eng, H, first=0, end=None):
            for step in range(first, H.n + 2 if end is None else end):
                h = step
                if h < H.n:
                    g = H.first + h
                    if g >= 2:
                        eng.wait_ge(s_exp, g - 1)
                    for qt in range(TT):
                        nk = P * (qt + 1) if H.causal else TOK
                        out = SB[:, g % 2, qt * TOK:qt * TOK + nk]
                        mm = [(H.q(h)[:, qt * P:(qt + 1) * P], H.k(h)[:, 0:nk], out)]
                        if H.forget:
                            mm.append((fcT[:, qt * P:(qt + 1) * P], ident[:, h:h + 1].to_broadcast([P, nk]), out))
                            mm.append((ident[:, h:h + 1].to_broadcast([P, P]), fcN[:, 0:nk], out))
                        if H.causal:
                            mm.append((ident[:, :], maskneg[:, :], SB[:, g % 2, qt * TOK + nk - P:qt * TOK + nk]))
                        for m, (l_, r_, o_) in enumerate(mm):
                            last = eng.matmul(o_, l_, r_, start=m == 0, stop=m == len(mm) - 1)
                    last.then_inc(s_sc, 1)
                h = step - 1
                if 0 <= h < H.n:
                    g = H.first + h
                    eng.wait_ge(s_p, g + 1)
                    if g >= 1:
                        eng.wait_ge(s_tc, g)
                    pr = H.p[h % 2]
                    eng.transpose(TB[:, 0:128], pr[:, 0, 0:128], ident[:, :])
                    eng.transpose(TB[:, 128:256], pr[:, 1, 0:128], ident[:, :])
                    if not H.causal:
                        eng.transpose(TB[:, 384:512], pr[:, 0, 128:256], ident[:, :])
                    eng.transpose(TB[:, 256:384], pr[:, 1, 128:256], ident[:, :]).then_inc(s_t, 1)
                h = step - 2
                if 0 <= h < H.n:
                    g = H.first + h
                    eng.wait_ge(s_tc, g + 1)
                    if g >= 1:
                        eng.wait_ge(s_tmp, g)
                    pt = H.t[h % 2]
                    eng.matmul(OB[:, 0:256], H.v(h, 0), pt[:, 0:256], start=True, stop=False)
                    if not H.causal:
                        eng.matmul(OB[:, 0:128], H.v(h, 1), pt[:, 384:512], start=False, stop=False)
                    eng.matmul(OB[:, 128:256], H.v(h, 1), pt[:, 256:384], start=False, stop=True).then_inc(s_o, 1)

        def act_heads(eng, H, first=0, end=None):
            for step in range(first, H.n + 2 if end is None else end):
                h = step
                if h < H.n:
                    g = H.first + h
                    eng.wait_ge(s_mx, g + 1)
                    if h >= 2:
                        eng.wait_ge(s_t, g - 1)
                    for qt in range(TT):
                        nk = P * (qt + 1) if H.causal else TOK
                        ins = eng.activation(H.p[h % 2][:, qt, 0:nk], SB[:, g % 2, qt * TOK:qt * TOK + nk], ACT.Exp,
                                             bias=nmax[:, g % 2, qt:qt + 1], accum_out=psumr[:, g % 2, qt:qt + 1])
                    ins.then_inc(s_exp, 1)
                h = step - 1
                if 0 <= h < H.n:
                    g = H.first + h
                    eng.wait_ge(s_t, g + 1)
                    if h >= 2:
                        eng.wait_ge(s_o, g - 1)
                    n = 384 if H.causal else 512
                    eng.activation(H.t[h % 2][:, 0:n], TB[:, 0:n], ACT.Copy).then_inc(s_tc, 1)
                h = step - 2
                if 0 <= h < H.n:
                    g = H.first + h
                    if H.out0 is None:
                        continue
                    eng.wait_ge(s_tmp, g + 1)
                    eng.activation(ah[:, H.out0 + h, :], rstd[:, :], ACT.Copy).then_inc(s_hi, 1)

        def dve_heads(eng, H, first=0, end=None):
            def maxima(h):
                if h < H.n:
                    g = H.first + h
                    eng.wait_ge(s_sc, g + 1)
                    if g >= 2:
                        eng.wait_ge(s_exp, g - 1)
                    for qt in range(TT):
                        nk = P * (qt + 1) if H.causal else TOK
                        ins = eng.tensor_reduce(nmax[:, g % 2, qt:qt + 1], SB[:, g % 2, qt * TOK:qt * TOK + nk],
                                                AX.X, ALU.max, negate=True)
                    ins.then_inc(s_mx, 1)

            def probabilities(h):
                if 0 <= h < H.n:
                    g = H.first + h
                    eng.wait_ge(s_exp, g + 1)
                    eng.reciprocal(pinv[:, g % 2, :], psumr[:, g % 2, :]).then_inc(s_inv, 1)
                    eng.wait_ge(s_inv, g + 1)
                    for qt in range(TT):
                        nk = P * (qt + 1) if H.causal else TOK
                        pr = H.p[h % 2][:, qt, 0:nk]
                        ins = eng.tensor_scalar(pr, pr, pinv[:, g % 2, qt:qt + 1], None, ALU.mult)
                    ins.then_inc(s_p, 1)

            for step in range(first, H.n + 2 if end is None else end):
                probabilities(step - 1)
                maxima(step)
                h = step - 2
                if 0 <= h < H.n:
                    g = H.first + h
                    eng.wait_ge(s_o, g + 1)
                    if H.out0 is None:
                        eng.tensor_copy(H.q(h), OB[:, 0:256]).then_inc(s_tmp, 1)
                        continue
                    if h >= 1:
                        eng.wait_ge(s_lo, H.cut + h)
                    if H.gate is None:
                        ins = eng.tensor_copy(rstd[:, :], OB[:, 0:256])
                    else:
                        ins = eng.tensor_tensor(rstd[:, :], OB[:, 0:256], H.gate(h), ALU.mult)
                    ins.then_inc(s_tmp, 1)
                    eng.wait_ge(s_hi, H.cut + h + 1)
                    eng.tensor_tensor(al[:, H.out0 + h, :], rstd[:, :], ah[:, H.out0 + h, :].bitcast(F32),
                                      ALU.subtract).then_inc(s_lo, 1)

        def tok_v(t):
            return lambda h, kt: t[:, kt, h * P:(h + 1) * P]

        slot_tok = lambda s, n: rflat[:, s, :].rearrange("p (a n) -> p a n", a=2)
        fox = Heads(0, HH, lambda h: ablk[:, 32 + h, :], lambda h: ablk[:, 40 + h, :], tok_v(slot_tok(6, HG)),
                    True, None, ringscr[:, 0:SLOT], forget=True)
        memA = flat[:, 0:SLOT]
        heads_a = Heads(8, MH, lambda h: ablk[:, 24 + h, :], lambda h: memA[:, h * TOK:(h + 1) * TOK],
                        tok_v(memA[:, 1024:2048].rearrange("p (a n) -> p a n", a=2)),
                        False, None, (sflat[:, 12 * TOK:16 * TOK], flat[:, 8 * TOK:12 * TOK]))
        memB = flat[:, 0:SLOT]
        heads_b = Heads(24, MH, lambda h: ablk[:, 48 + h, :], lambda h: memB[:, h * TOK:(h + 1) * TOK],
                        tok_v(memB[:, 1024:2048].rearrange("p (a n) -> p a n", a=2)),
                        False, BB, flat[:, SLOT:2 * SLOT], gate=lambda h: ablk[:, 52 + h, :], cut=0)
        vshared = flat[:, 12 * TOK:24 * TOK].rearrange("p (a n) -> p a n", a=2)
        moba = Heads(12, BB, lambda h: ablk[:, 24 + h, :], lambda h: ablk[:, h, :], tok_v(vshared),
                     True, None, flat[:, 48 * TOK:48 * TOK + SLOT])

        W = PAD + TOK
        pads = [flat[:, 24 * TOK + b * PG * W:24 * TOK + (b + 1) * PG * W].rearrange("p (a t) -> p a t", a=PG)
                for b in range(2)]

        def pool_out(g):
            return pads[g % 2][:, :, PAD:W]

        T = [scr[:, s, :] for s in range(4)]
        V_TOK = slot_tok(2, HG)

        def head(t, h):
            return t[:, h * TOK:(h + 1) * TOK]

        attn_sb = [T[0][:, 256 * b:256 * b + 256] for b in range(2)]
        kend_sb = [T[0][:, 512 + 384 * b:896 + 384 * b] for b in range(2)]
        state = [T[0][:, 1280 + 384 * b:1664 + 384 * b].rearrange("p (a b) -> p a b", a=3) for b in range(2)]
        QD, KE, GS, OUT = rflat[:, 0, :], rflat[:, 1, :], rflat[:, 3, :], rflat[:, 0, :]
        KD = T[3]

        block = ctx.enter_context(nc.Block())

        @block.sync
        def _(sp):
            rows = ((A["norm1"], 0, 0, 16), (A["norm2"], 0, 16, 16), (A["final"], 0, 32, 16), (A["ln_g"], 0, 48, 32),
                    (A["ln_b"], 0, 80, 32), (A["pool_scale"], 0, 112, 12), (A["conv_w"][0:2], 1, 0, 88),
                    (A["lbp"], 1, 88, 16), (A["hgain"], 1, 104, 1), (A["conv_w"][2:3], 2, 0, 44), (A["conv_b"], 2, 44, 44))
            for j in range(2):
                sp.dma_start(memtok[:, j, :], A["mem"][j * P:(j + 1) * P, :]).then_inc(mem_loaded, 16)
            for v, tile, r0, n in rows:
                src = v.rearrange("a (r p) -> (a r) p", p=P)
                sp.dma_start(vrows[r0:r0 + n, tile, :], src).then_inc(vec_loaded, 16)
            sp_phase(sp, "mem_k0")
            for j in range(2):
                sp.dma_start(xtok[:, j, :], A["x"][j * P:(j + 1) * P, :]).then_inc(x_loaded, 16)
            for p in order[1:]:
                sp_phase(sp, p.name)
            for j in range(TT):
                sp.wait_ge(o_sb, 4 * (j + 1))
                sp.dma_start(A["result"][j * P:(j + 1) * P, :], sflat[:, j * D:(j + 1) * D]).then_inc(out_stored, 16)
            sp.wait_ge(out_stored, 32)

        @block.gpsimd
        def _(pool):
            count = [0]

            def link(ins):
                count[0] += 1
                ins.then_inc(pool_seq, 1)
                pool.wait_ge(pool_seq, count[0])

            link(pool.memset(meanw[:, :], 1.0 / D))
            link(pool.memset(epsr[:, :], EPS))
            link(pool.memset(epsl[:, :], LN_EPS))
            link(pool.memset(one1[:, :], 1.0))
            for t in range(PAD):
                link(pool.memset(invcnt[:, t:t + 1], 1.0 / (t + 1)))
            link(pool.memset(maskneg[:, :], 0.0))
            link(pool.memset(tri01[:, :], 1.0))
            link(pool.memset(scanmask[:, :], 1.0))
            link(pool.memset(scanmask[:, :].rearrange("p (n c) -> p n c", c=CHUNK)[:, :, 0:1], 0.0))
            link(pool.memset(ident[:, :], 0.0))
            link(pool.affine_select(out=maskneg[:, :], in_=maskneg[:, :], compare_op=ALU.is_ge, fill=NEG, base=0,
                                    pattern=[[-1, P]], channel_multiplier=1))
            link(pool.affine_select(out=tri01[:, :], in_=tri01[:, :], compare_op=ALU.is_ge, fill=0.0, base=0,
                                    pattern=[[1, P]], channel_multiplier=-1))
            link(pool.tensor_copy(chunktri[:, :], tri01[:, :]))
            link(pool.memset(chunktri[0:CHUNK, CHUNK:P], 0.0))
            pool.affine_select(out=ident[:, :], in_=ident[:, :], compare_op=ALU.not_equal, fill=1.0, base=0,
                               pattern=[[-1, P]], channel_multiplier=1).then_inc(consts, 1)
            link(pool.memset(fbias[:, :], 0.0))
            pool.dma_start(fbias[0:HH, :], A["fox_bias"].rearrange("a h -> h a")).then_inc(fb_loaded, 16)
            pool.dma_start(fwraw[:, :, :], A["w_in"][:, 7 * HG:7 * HG + HH].rearrange("(t p) n -> p t n", p=P))\
                .then_inc(fw_loaded, 16)
            for l in range(2):
                phase_over(pool, f"mem_v{l}")
                pool.dma_start(memkv[l], stage[:, :]).then_inc(stored, 16)
            pool.wait_ge(n_lo, 4)
            pool.memset(fwhi[:, :, :].bitcast(F32), 0.0).then_inc(fw_zero, 1)
            pool.memset(fwlo[:, :, :].bitcast(F32), 0.0).then_inc(fw_zero, 1)
            pool.wait_ge(stored, 32)
            pool.wait_ge(p_lo, 4)
            pool.dma_start(memA, memkv[0]).then_inc(reloaded, 16)
            pool_norm_bias(pool, 3)
            pool.wait_ge(s_o, 24)
            pool.dma_start(memB, memkv[1]).then_inc(reloaded, 16)
            pool_norm_bias(pool, 4)

        @block.tensor
        def _(pe):
            pe.wait_ge(consts, 1)
            turn = 0

            def transposes(src, loaded, done_sems):
                nonlocal turn
                for g in range(8):
                    if turn >= 4:
                        prev = turn - 4
                        if prev < 8:
                            pe.wait_ge(mem_lo, prev + 1)
                        else:
                            pe.wait_ge(x_ready, prev - 7)
                    for k in range(2):
                        for t in range(TT):
                            kk = 2 * g + k
                            last = pe.transpose(XP[turn % 4][:, k * 256 + t * P:k * 256 + (t + 1) * P],
                                                src[:, t, kk * P:(kk + 1) * P], ident[:, :])
                    last.then_inc(in_t, 1)
                    turn += 1

            pe.wait_ge(mem_loaded, 32)
            transposes(memtok, None, None)
            pe.wait_ge(x_loaded, 32)
            transposes(xtok, None, None)
            pe.wait_ge(vec_loaded, 11 * 16)
            pe.wait_ge(x_ready, 5)
            for v, n in enumerate((124, 105, 88)):
                last = pe.transpose(XP[0][:, v * P:v * P + n], vrows[0:n, v, :], ident[0:n, 0:n])
            last.then_inc(vec_t, 1)
            pe.wait_ge(mem_lo, 8)
            pe_phase(pe, "mem_k0")
            pe.wait_ge(x_ready, 8)
            pe_norm(pe, 0)
            for n in ("mem_v0", "mem_k1", "mem_v1"):
                pe_phase(pe, n)
            pe_phase(pe, "in_qf", norm=0)
            pe.wait_ge(fw_lo, 1)
            for k in range(KT):
                for r, (l_, r_) in enumerate(((fwhi[:, k, :], ah[:, k, :]), (fwhi[:, k, :], al[:, k, :]),
                                              (fwlo[:, k, :], ah[:, k, :]))):
                    last = pe.matmul(TB[:, 0:TOK], l_, r_, start=k == 0 and r == 0, stop=k == KT - 1 and r == 2)
            last.then_inc(fg_done, 1)
            for n in ("in_i", "in_gqk", "in_v"):
                pe_phase(pe, n)
            phase_over(pe, "in_v")

            def recur(step):
                h = step
                if h < HH:
                    if h >= 2:
                        pe.wait_ge(r_attn, h)
                    bank = G[:, h % 2, :]
                    for t in range(TT):
                        c = slice(t * P, (t + 1) * P)
                        pe.matmul(bank[:, t * P:(t + 1) * P], head(KD, h)[:, c], head(QD, h)[:, c], start=True, stop=True)
                        last = pe.transpose(bank[:, 256 + t * P:256 + (t + 1) * P], head(KE, h)[:, c], ident[:, :])
                    last.then_inc(r_a, 1)
                h = step - 1
                if 0 <= h < HH:
                    pe.wait_ge(r_kt, h + 1)
                    if h >= 1:
                        pe.wait_ge(r_state, 3 * h)
                    for n in range(NCH - 1):
                        c = (0, 2, 1)[n] * P
                        last = pe.matmul(G[:, 2, n * P:(n + 1) * P], kend_sb[h % 2][:, c:c + P],
                                         V_TOK[:, n // 2, h * P:(h + 1) * P], start=True, stop=True)
                    last.then_inc(r_kv, 1)
                h = step - 2
                if 0 <= h < HH:
                    pe.wait_ge(r_state, 3 * (h + 1))
                    pe.wait_ge(r_attn, h + 2)
                    if h >= 1:
                        pe.wait_ge(r_oev, h)
                    for t in range(TT):
                        pe.matmul(G[:, 3, t * P:(t + 1) * P], V_TOK[:, t, h * P:(h + 1) * P],
                                  attn_sb[h % 2][:, t * P:(t + 1) * P], start=True, stop=False)
                        for n in range(max(1, 2 * t), 2 * t + 2):
                            c = slice(n * CHUNK, (n + 1) * CHUNK)
                            last = pe.matmul(G[:, 3, c], state[h % 2][:, n - 1, :], head(QD, h)[:, c],
                                             start=False, stop=n % 2 == 1)
                    last.then_inc(r_o, 1)
            pe.wait_ge(fg_seq, 7)
            pe_heads(pe, fox, 0, 4)
            pe.wait_ge(r_attn, 1)
            for step in range(HH + 2):
                pe_heads(pe, fox, 4 + step, min(5 + step, HH + 2))
                recur(step)
            for b in range(4):
                pe.wait_ge(r_sq, 2 * (b + 1))
                pe.matmul(G[:, b, :], meanw[:, :], rflat[:, 1, b * 512:(b + 1) * 512], start=True, stop=True)\
                    .then_inc(r_stat, 1)
            pe_phase(pe, "out", halves=(((r_lo, 4),), ((f_lo, 1),)))
            pe_norm(pe, 1)
            for half in range(2):
                pe_phase(pe, f"ffn{half}", norm=1)
                pe_phase(pe, f"down{half}")
            pe_norm(pe, 2)
            for n in ("in0_branch", "in0_gate", "in0"):
                pe_phase(pe, n, norm=2)
            phase_over(pe, "in0")
            pe.wait_ge(p_lo, 4)
            pe.wait_ge(reloaded, 16)
            pe.wait_ge(q_scaled, 1)
            pe_phase(pe, "pool", between=lambda m: pe_heads(pe, heads_a, m, min(m + 1, MH + 2)))
            pe_phase(pe, "out0", halves=(((pm_l, 4),), ((pm_l, 6), (a_lo, 1))))
            pe_norm(pe, 3)
            for n in ("kvs_k", "kvs_v", "in1_q"):
                pe_phase(pe, n, norm=3)
            phase_over(pe, "in1_q")
            pe.wait_ge(q_scaled, 2)
            pe_phase(pe, "in1_gate", between=lambda m: pe_heads(pe, moba, m, m + 1))
            pe_heads(pe, moba, BB)
            pe_phase(pe, "in1")
            pe.wait_ge(reloaded, 32)
            pe.wait_ge(q_scaled, 3)
            pe_heads(pe, heads_b)
            pe_phase(pe, "out1", halves=(((b_lo, 3),), ((b_lo, 4), (s_lo, 4))))
            pe_norm(pe, 4)
            for t in range(TT):
                for q in range(4):
                    n = 4 * t + q
                    if t == 0:
                        pe.wait_ge(n_b, 4 + q + 1)
                    if n >= 4:
                        pe.wait_ge(o_sb, n - 3)
                    for k in range(4):
                        last = pe.transpose(G[:, n % 4, k * P:(k + 1) * P], xres[:, 4 * q + k, t * P:(t + 1) * P], ident[:, :])
                    last.then_inc(o_t, 1)

        @block.scalar
        def _(act):
            splits(act, True, order[0], 0, 0)
            for g in range(8):
                act.wait_ge(in_t, g + 1)
                act.activation(memh[:, 2 * g:2 * g + 2, :], blocks(XP[g % 4]), ACT.Copy).then_inc(mem_hi, 1)
            for g in range(8):
                act.wait_ge(in_t, g + 9)
                act.activation(xres[:, 2 * g:2 * g + 2, :], blocks(XP[g % 4]), ACT.Copy).then_inc(x_ready, 1)
            act.wait_ge(x_ready, 8)
            act.wait_ge(vec_t, 1)
            act_norm_squares(act, 0)

            def kv_evict(name, token):
                p = phases[name]

                def evict(i, cb):
                    chunk_wait(act, p, i, cb)
                    if name in ("mem_k1",):
                        act.wait_ge(stored, 16)
                    if token:
                        dst = stage[:, 1024:2048].rearrange("p (a n) -> p a n", a=2)[:, :, cb * 256:(cb + 1) * 256]
                    else:
                        dst = blocks(stage[:, cb * 512:(cb + 1) * 512])
                    act.activation(dst, G[:, 2 * cb:2 * cb + 2, 0:256], ACT.Copy).then_inc(pair_free[cb], 1)
                return evict

            cut_phase(act, True, "mem_k0", kv_evict("mem_k0", False))
            act_norm_scale(act, 0)
            act_norm_out(act, 0, quarters=(0, 1))
            act.wait_ge(lb_chain, 3)
            act.activation(lbt[:, 2:4, :], lbt[:, 0:2, :], ACT.Exp).then_inc(lb_exp, 1)
            cut_phase(act, True, "mem_v0", kv_evict("mem_v0", True))
            act_norm_out(act, 0, quarters=(1, 2))
            cut_phase(act, True, "mem_k1", kv_evict("mem_k1", False))
            act_norm_out(act, 0, quarters=(2, 4))
            cut_phase(act, True, "mem_v1", kv_evict("mem_v1", True))
            act.wait_ge(fw_loaded, 16)
            act.wait_ge(fw_zero, 2)
            act.activation(fwhi[:, :, 0:HH], fwraw[:, :, :], ACT.Copy).then_inc(fw_hi, 1)
            cut_phase(act, True, "in_qf", copy_evict(act, "in_qf", 0))
            phase_over(act, "in_qf")
            act.activation(rflat[:, 1, :], rflat[:, 1, :], ACT.Sigmoid).then_inc(g_sig, 1)
            cut_phase(act, True, "in_i", token_evict(act, "in_i", V_TOK))
            cut_phase(act, True, "in_gqk", copy_evict(act, "in_gqk", 24))
            phase_over(act, "in_gqk")
            act.activation(GS, GS, ACT.Silu).then_inc(g_act, 1)
            act.wait_ge(stored, 32)
            cut_phase(act, True, "in_v", token_evict(act, "in_v", slot_tok(6, HG)))
            phase_over(act, "in_v")
            act.wait_ge(fg_seq, 2)
            act.activation(fe, fcT, ACT.Exp, scale=-1.0).then_inc(fg_act, 1)
            act.wait_ge(fg_act, 1)
            act.activation(fe, fe, ACT.Ln, bias=one1[:, 0:1]).then_inc(fg_act, 1)
            act.wait_ge(g_seq, 1)
            act.activation(T[0], rflat[:, 1, :], ACT.Ln).then_inc(g_act, 1)
            act_heads(act, fox, 0, 1)
            act.wait_ge(g_seq, 10)
            act.activation(T[0], T[2], ACT.Exp).then_inc(g_act, 1)
            act_heads(act, fox, 1, 2)
            act.wait_ge(g_seq, 12)
            act.activation(T[0], T[2], ACT.Exp, scale=-1.0).then_inc(g_act, 1)
            act_heads(act, fox, 2, 3)
            act.wait_ge(g_seq, 14)
            act.activation(T[0], T[0], ACT.Exp).then_inc(g_act, 1)
            act_heads(act, fox, 3, 4)
            for step in range(HH + 2):
                act_heads(act, fox, 4 + step, min(5 + step, HH + 2))
                h = step
                if h < HH:
                    act.wait_ge(r_a, h + 1)
                    if h >= 2:
                        act.wait_ge(r_kv, h - 1)
                    act.activation(kend_sb[h % 2][0:CHUNK, 0:256], G[0:CHUNK, h % 2, 256:512], ACT.Copy)
                    act.activation(kend_sb[h % 2][CHUNK:P, 256:384], G[CHUNK:P, h % 2, 256:384], ACT.Copy)\
                        .then_inc(r_kt, 1)
                h = step - 2
                if 0 <= h < HH:
                    act.wait_ge(r_o, h + 1)
                    act.activation(head(OUT, h), G[:, 3, 0:256], ACT.Copy).then_inc(r_oev, 1)
                    act.wait_ge(r_oev, h + 1)
                    act.activation(head(KE, h), head(OUT, h), ACT.Square).then_inc(r_sq, 1)
            act.wait_ge(s_tmp, HH)
            act.activation(ah[:, HH:KT, :], ablk[:, 32:40, :], ACT.Copy).then_inc(f_hi, 1)
            for b in range(4):
                act.wait_ge(r_stat, b + 1)
                act.activation(T[0][:, b * 512:(b + 1) * 512], G[:, b, :], ACT.Ln, bias=epsr[:, 0:1],
                               scale=float(D // P)).then_inc(r_ln, 1)
            for b in range(4):
                act.wait_ge(r_ln, b + 1)
                quarter = T[0][:, b * 512:(b + 1) * 512]
                act.activation(quarter, quarter, ACT.Exp, scale=-0.5).then_inc(r_rstd, 1)
            for b in range(4):
                act.wait_ge(r_seq, 2 * (b + 1))
                act.activation(ah[:, 2 * b:2 * b + 2, :], ablk[:, 2 * b:2 * b + 2, :], ACT.Copy).then_inc(r_hi, 1)
            cut_phase(act, True, "out", squares_evict(act, "out", 1))
            act_norm_scale(act, 1)
            act_norm_out(act, 1)

            def ffn_evict(name):
                p = phases[name]
                b0 = int(name[-1]) * (HB // 2)

                def evict(i, cb):
                    n = i + b0
                    if cb == 0:
                        chunk_wait(act, p, i, 0)
                        act.wait_ge(conv_cur, n + 1)
                        for b in range(2):
                            act.activation(cbuf[:, b, :], G[:, b, 0:256], ACT.Identity, scale=convc[:, b, 2:3],
                                           bias=convc[:, b, 3:4]).then_inc(conv_c, 1)
                    else:
                        left_wait(act, p, i, 0)
                        act.activation(sbuf_[:, :, :], cbuf[:, :, :], ACT.Silu).then_inc(conv_s, 1)
                        left_wait(act, p, i, 1)
                        act.activation(hh[:, ds(i * 2, 2), :], hv[:, :, :], ACT.Copy).then_inc(h_hi, 1)
                return evict

            for half in range(2):
                cut_phase(act, True, f"ffn{half}", ffn_evict(f"ffn{half}"))
                cut_phase(act, True, f"down{half}", squares_evict(act, "down1", 2) if half else no_evict)
            act_norm_scale(act, 2)
            act_norm_out(act, 2)
            cut_phase(act, True, "in0_branch", copy_evict(act, "in0_branch", 0))

            def pool_hi(m):
                if m % 3 == 0:
                    g = m // 3
                    act.wait_ge(p_hi, 2 * g + 1)
                    act.activation(ph_[:, PG * g:PG * g + PG, :], pool_out(g), ACT.Copy).then_inc(p_hi, 1)

            cut_phase(act, True, "in0_gate", copy_evict(act, "in0_gate", 12), between=pool_hi)
            act.wait_ge(p_lo, 4)
            cut_phase(act, True, "in0", copy_evict(act, "in0", 24))
            phase_over(act, "in0")
            act.activation(ablk[:, 12:24, :], ablk[:, 12:24, :], ACT.Silu).then_inc(silu_done, 1)
            act.activation(ablk[:, 28:32, :], ablk[:, 28:32, :], ACT.Silu).then_inc(silu_done, 1)

            def pool_evict(i, cb):
                c = 2 * i + cb
                left_wait(act, phases["pool"], i, cb)
                act.activation(ah[:, 2 * c:2 * c + 2, :], blocks(sflat[:, 28 * TOK:30 * TOK]), ACT.Copy).then_inc(pm_h, 1)

            cut_phase(act, True, "pool", pool_evict,
                      between=lambda m: act_heads(act, heads_a, m, min(m + 1, MH + 2)))
            act.wait_ge(a_val, 1)
            act.activation(ah[:, BB:KT, :], ablk[:, 24:28, :], ACT.Copy).then_inc(a_hi, 1)
            cut_phase(act, True, "out0", no_evict)
            act_norm_squares(act, 3)
            act_norm_scale(act, 3)
            act_norm_out(act, 3)
            cut_phase(act, True, "kvs_k", copy_evict(act, "kvs_k", 0))
            cut_phase(act, True, "kvs_v", token_evict(act, "kvs_v", vshared))
            cut_phase(act, True, "in1_q", copy_evict(act, "in1_q", 24))
            cut_phase(act, True, "in1_gate", copy_evict(act, "in1_gate", 36),
                      between=lambda m: act_heads(act, moba, m, m + 1))
            act_heads(act, moba, BB)
            phase_over(act, "in1_gate")
            act.activation(ablk[:, 36:48, :], ablk[:, 36:48, :], ACT.Silu).then_inc(silu_done, 1)
            act.wait_ge(s_o, 24)
            cut_phase(act, True, "in1", copy_evict(act, "in1", 48))
            phase_over(act, "in1")
            act.activation(ablk[:, 52:56, :], ablk[:, 52:56, :], ACT.Silu).then_inc(silu_done, 1)
            for q in range(MH + 2):
                act_heads(act, heads_b, q, q + 1)
                if q < 4:
                    act.wait_ge(b_val, q + 1)
                    act.activation(ah[:, 3 * q:3 * q + 3, :], ablk[:, 24 + 3 * q:27 + 3 * q, :],
                                   ACT.Copy).then_inc(b_hi, 1)
            cut_phase(act, True, "out1", no_evict)
            act_norm_squares(act, 4)
            act_norm_scale(act, 4)
            act_norm_out(act, 4, split=False)
            for n in range(0, 8, 2):
                act.wait_ge(o_t, n + 1)
                if n:
                    act.wait_ge(o_sb, n)
                act.activation(sflat[:, n * 512:(n + 1) * 512], G[:, n % 4, :], ACT.Copy).then_inc(o_sb, 1)

        @block.vector
        def _(dve):
            counts = {}

            def link(sm, ins):
                key = sm.name
                counts[key] = counts.get(key, 0) + 1
                ins.then_inc(sm, 1)
                dve.wait_ge(sm, counts[key])

            dve.wait_ge(consts, 1)
            splits(dve, False, order[0], 0, 0)
            for g in range(8):
                dve.wait_ge(mem_hi, g + 1)
                dve.tensor_tensor(meml[:, 2 * g:2 * g + 2, :], blocks(XP[g % 4]),
                                  memh[:, 2 * g:2 * g + 2, :].bitcast(F32), ALU.subtract).then_inc(mem_lo, 1)
            dve.wait_ge(vec_t, 1)
            dve.tensor_copy(colv[:, 0:124], XP[0][:, 0:124])
            dve.tensor_copy(colv[:, 124:229], XP[0][:, P:P + 105])
            link(vec_ready, dve.tensor_copy(colv[:, 229:317], XP[0][:, 2 * P:2 * P + 88]))
            dve.tensor_copy(convp[:, :, 0:2], colv[:, 124:212].rearrange("p (j b) -> p b j", j=2))
            dve.tensor_copy(convp[:, :, 2:4], colv[:, 229:317].rearrange("p (j b) -> p b j", j=2))
            p0, p1 = colv[:, 212:220], colv[:, 220:228]
            link(lb_chain, dve.tensor_tensor(lbt[:, 2, :], p0, p1, ALU.max))
            dve.tensor_tensor(lbt[:, 0, :], p0, lbt[:, 2, :], ALU.subtract).then_inc(lb_chain, 1)
            dve.tensor_tensor(lbt[:, 1, :], p1, lbt[:, 2, :], ALU.subtract).then_inc(lb_chain, 1)
            counts[lb_chain.name] = 3
            cut_phase(dve, False, "mem_k0", no_evict)
            dve_norm(dve, 0, quarters=(0, 1))
            dve.wait_ge(lb_exp, 1)
            link(lb_chain, dve.tensor_tensor(lbt[:, 0, :], lbt[:, 2, :], lbt[:, 3, :], ALU.add))
            link(lb_chain, dve.reciprocal(lbt[:, 1, :], lbt[:, 0, :]))
            link(lb_chain, dve.tensor_tensor(lb[:, :], lbt[:, 2, :], lbt[:, 1, :], ALU.mult))
            link(lb_chain, dve.tensor_scalar(omlb[:, :], lb[:, :], -1.0, 1.0, ALU.mult, ALU.add))
            cut_phase(dve, False, "mem_v0", no_evict)
            dve_norm(dve, 0, quarters=(1, 2))
            cut_phase(dve, False, "mem_k1", no_evict)
            dve_norm(dve, 0, quarters=(2, 5))
            cut_phase(dve, False, "mem_v1", no_evict)
            dve.wait_ge(fw_hi, 1)
            dve.tensor_tensor(fwlo[:, :, 0:HH], fwraw[:, :, :], fwhi[:, :, 0:HH].bitcast(F32), ALU.subtract).then_inc(fw_lo, 1)
            cut_phase(dve, False, "in_qf", no_evict)
            cut_phase(dve, False, "in_i", no_evict)
            dve.wait_ge(g_sig, 1)
            for h in range(HH):
                f = head(rflat[:, 1, :], h)
                ins = dve.tensor_scalar(f, f, omlb[:, h:h + 1], lb[:, h:h + 1], ALU.mult, ALU.add)
            link(g_seq, ins)
            for n in ("in_gqk", "in_v"):
                cut_phase(dve, False, n, no_evict)
            phase_over(dve, "in_v")
            dve.wait_ge(fg_done, 1)
            dve.wait_ge(fb_loaded, 16)
            link(fg_seq, dve.tensor_scalar(fx, TB[:, 0:TOK], fbias[:, 0:1], None, ALU.add))
            link(fg_seq, dve.scalar_tensor_tensor(fcT, fx, -1.0, fx, ALU.mult, ALU.max))
            link(fg_seq, dve.memset(ones, 1.0))
            dve.wait_ge(fg_act, 2)
            link(fg_seq, dve.scalar_tensor_tensor(fx, fx, 0.0, fe, ALU.min, ALU.subtract))
            link(fg_seq, dve.tensor_tensor_scan(fcT, ones, fx, 0.0, ALU.mult, ALU.add))
            link(fg_seq, dve.tensor_scalar(fcN, fcT, -1.0, None, ALU.mult))
            dve.tensor_scalar(rflat[:, 4, :], rflat[:, 4, :], SCALE, None, ALU.mult).then_inc(fg_seq, 1)
            link(g_seq, dve.tensor_scalar(T[1], rflat[:, 1, :], -1.0, 1.0, ALU.mult, ALU.add))
            dve_heads(dve, fox, 0, 1)
            dve.wait_ge(g_act, 2)
            for h in range(HH):
                dve.tensor_tensor_scan(head(T[2], h), scanmask[:, :], head(T[0], h), 0.0,
                                       ALU.mult, ALU.add).then_inc(g_seq, 1)
            dve_heads(dve, fox, 1, 2)
            dve.wait_ge(g_act, 3)
            dve.tensor_copy(decay[:, :, :], T[0].rearrange("p (h n c) -> p h n c", h=HH, c=CHUNK)[:, :, :, CHUNK - 1])\
                .then_inc(g_seq, 1)
            dve.scalar_tensor_tensor(QD, QD, SCALE, T[0], ALU.mult, ALU.mult).then_inc(g_seq, 1)
            dve_heads(dve, fox, 2, 3)
            dve.wait_ge(g_act, 4)
            dve.tensor_tensor(KD, T[1], T[0], ALU.mult).then_inc(g_seq, 1)
            b4 = T[2].rearrange("p (n c) -> p n c", c=CHUNK)
            dve.wait_ge(g_seq, 13)
            dve.tensor_tensor(T[0].rearrange("p (n c) -> p n c", c=CHUNK),
                              b4[:, :, CHUNK - 1:CHUNK].broadcast_to([P, HH * NCH, CHUNK]), b4, ALU.subtract).then_inc(g_seq, 1)
            dve_heads(dve, fox, 3, 4)
            dve.wait_ge(g_act, 5)
            dve.tensor_tensor(KE, T[1], T[0], ALU.mult).then_inc(g_seq, 1)
            dve.wait_ge(g_seq, 15)
            dve.memset(T[0][:, 0:1280], 0.0).then_inc(r_attn, 1)
            dve.wait_ge(r_attn, 1)

            for step in range(HH + 2):
                dve_heads(dve, fox, 4 + step, min(5 + step, HH + 2))
                h = step
                if h < HH:
                    dve.wait_ge(r_kt, h + 1)
                    if h >= 2:
                        dve.wait_ge(r_o, h - 1)
                    dve.copy_predicated(attn_sb[h % 2].rearrange("p (a b) -> p a b", a=2),
                                        chunktri[:, :].bitcast(U32).unsqueeze(1).broadcast_to([P, 2, P]),
                                        G[:, h % 2, 0:256].rearrange("p (a b) -> p a b", a=2)).then_inc(r_attn, 1)
                h = step - 1
                if 0 <= h < HH:
                    dve.wait_ge(r_kv, h + 1)
                    if h >= 2:
                        dve.wait_ge(r_o, h - 1)
                    st = state[h % 2]
                    dve.tensor_copy(st[:, 0, :], G[:, 2, 0:P]).then_inc(r_state, 1)
                    for n in (1, 2):
                        dve.wait_ge(r_state, 3 * h + n)
                        dve.scalar_tensor_tensor(st[:, n, :], st[:, n - 1, :], decay[:, h, n:n + 1],
                                                 G[:, 2, n * P:(n + 1) * P], ALU.mult, ALU.add).then_inc(r_state, 1)
            dve.wait_ge(f_hi, 1)
            dve.tensor_tensor(al[:, HH:KT, :], ablk[:, 32:40, :], ah[:, HH:KT, :].bitcast(F32), ALU.subtract).then_inc(f_lo, 1)
            for b in range(5):
                if b < 4:
                    c = slice(b * 512, (b + 1) * 512)
                    dve.wait_ge(r_rstd, b + 1)
                    link(r_seq, dve.scalar_tensor_tensor(OUT[:, c], OUT[:, c], colv[:, 228:229], T[0][:, c],
                                                         ALU.mult, ALU.mult))
                    link(r_seq, dve.tensor_tensor(OUT[:, c], OUT[:, c], GS[:, c], ALU.mult))
                if b:
                    k = slice(2 * b - 2, 2 * b)
                    dve.wait_ge(r_hi, b)
                    dve.tensor_tensor(al[:, k, :], ablk[:, k, :], ah[:, k, :].bitcast(F32), ALU.subtract)\
                        .then_inc(r_lo, 1)
            cut_phase(dve, False, "out", residual_evict(dve, "out", norm=1))
            dve_norm(dve, 1)

            def ffn_evict(name):
                p = phases[name]
                b0 = int(name[-1]) * (HB // 2)

                def evict(i, cb):
                    n = i + b0
                    if cb == 0:
                        dve.tensor_copy(convc[:, :, :], convp[:, ds(i * 2 + 2 * b0, 2), :]).then_inc(conv_cur, 1)
                        dve.wait_ge(conv_cur, n + 1)
                        for b in range(2):
                            dve.wait_ge(conv_c, n * 2 + (b + 1))
                            dve.scalar_tensor_tensor(cbuf[:, b, 1:TOK], G[:, b, 0:TOK - 1], convc[:, b, 1:2],
                                                     cbuf[:, b, 1:TOK], ALU.mult, ALU.add).then_inc(conv_1, 1)
                        for b in range(2):
                            dve.wait_ge(conv_1, n * 2 + (b + 1))
                            ins = dve.scalar_tensor_tensor(cbuf[:, b, 2:TOK], G[:, b, 0:TOK - 2], convc[:, b, 0:1],
                                                           cbuf[:, b, 2:TOK], ALU.mult, ALU.add)
                        ins.then_inc(pair_free[0], 1)
                    else:
                        chunk_wait(dve, p, i, 1)
                        dve.wait_ge(conv_s, n + 1)
                        ins = dve.tensor_tensor(hv[:, :, :], sbuf_[:, :, :], G[:, 2:4, 0:256], ALU.mult)
                        ins.then_inc(pair_free[1], 1)
                        dve.wait_ge(h_hi, n + 1)
                        dve.tensor_tensor(hl[:, ds(i * 2, 2), :], hv[:, :, :], hh[:, ds(i * 2, 2), :].bitcast(F32),
                                          ALU.subtract).then_inc(h_lo, 1)
                return evict

            for half in range(2):
                cut_phase(dve, False, f"ffn{half}", ffn_evict(f"ffn{half}"))
                cut_phase(dve, False, f"down{half}", residual_evict(dve, f"down{half}", norm=2 if half else None))
            dve_norm(dve, 2)
            cut_phase(dve, False, "in0_branch", no_evict)
            phase_over(dve, "in0_branch")
            link(p_seq, dve.memset(flat[:, 24 * TOK:24 * TOK + 2 * PG * W], 0.0))

            def pool_group(m):
                if m % 3:
                    return
                g = m // 3
                w, src = WINDOWS[g], ablk[:, PG * g:PG * g + PG, :]
                link(p_seq, dve.tensor_copy(pads[0][:, :, PAD:W], src))
                cur, k = 0, 1
                while k < w:
                    link(p_seq, dve.tensor_tensor(pads[1 - cur][:, :, PAD:W], pads[cur][:, :, PAD:W],
                                                  pads[cur][:, :, PAD - k:W - k], ALU.add))
                    cur, k = 1 - cur, 2 * k
                pm = pool_out(g)
                link(p_seq, dve.tensor_scalar(pm, pads[cur][:, :, PAD:W], 1.0 / w, None, ALU.mult))
                link(p_seq, dve.tensor_tensor(pm[:, :, 0:w - 1], pads[cur][:, :, PAD:PAD + w - 1],
                                              invcnt[:, 0:w - 1].unsqueeze(1).broadcast_to([P, PG, w - 1]), ALU.mult))
                dve.tensor_tensor(pm, pm, src, ALU.subtract).then_inc(p_hi, 1)
                dve.wait_ge(p_hi, 2 * g + 2)
                dve.tensor_tensor(pl_[:, PG * g:PG * g + PG, :], pm, ph_[:, PG * g:PG * g + PG, :].bitcast(F32),
                                  ALU.subtract).then_inc(p_lo, 1)
                dve.wait_ge(p_lo, g + 1)

            cut_phase(dve, False, "in0_gate", no_evict, between=pool_group)
            cut_phase(dve, False, "in0", no_evict)
            phase_over(dve, "in0")
            dve.tensor_scalar(ablk[:, 24:28, :], ablk[:, 24:28, :], SCALE, None, ALU.mult).then_inc(q_scaled, 1)
            dve.wait_ge(silu_done, 2)
            pmix = blocks(sflat[:, 28 * TOK:30 * TOK])

            def pool_evict(i, cb):
                c = 2 * i + cb
                chunk_wait(dve, phases["pool"], i, cb)
                if c:
                    dve.wait_ge(pm_l, c)
                for b in range(2):
                    j = 2 * c + b
                    ins = dve.scalar_tensor_tensor(pmix[:, b, :], G[:, 2 * cb + b, 0:256], colv[:, 112 + j:113 + j],
                                                   ablk[:, 12 + j, :], ALU.mult, ALU.mult)
                ins.then_inc(pair_free[cb], 1)
                dve.wait_ge(pm_h, c + 1)
                dve.tensor_tensor(al[:, 2 * c:2 * c + 2, :], pmix, ah[:, 2 * c:2 * c + 2, :].bitcast(F32),
                                  ALU.subtract).then_inc(pm_l, 1)

            cut_phase(dve, False, "pool", pool_evict,
                      between=lambda m: dve_heads(dve, heads_a, m, min(m + 1, MH + 2)))
            dve.wait_ge(s_tmp, 12)
            dve.tensor_tensor(ablk[:, 24:28, :], ablk[:, 24:28, :], ablk[:, 28:32, :], ALU.mult).then_inc(a_val, 1)
            dve.wait_ge(a_hi, 1)
            dve.tensor_tensor(al[:, BB:KT, :], ablk[:, 24:28, :], ah[:, BB:KT, :].bitcast(F32), ALU.subtract).then_inc(a_lo, 1)
            cut_phase(dve, False, "out0", residual_evict(dve, "out0", ALPHA, norm=3))
            dve_norm(dve, 3)
            for n in ("kvs_k", "kvs_v", "in1_q"):
                cut_phase(dve, False, n, no_evict)
            phase_over(dve, "in1_q")
            dve.tensor_scalar(ablk[:, 24:36, :], ablk[:, 24:36, :], SCALE, None, ALU.mult).then_inc(q_scaled, 1)
            cut_phase(dve, False, "in1_gate", no_evict, between=lambda m: dve_heads(dve, moba, m, m + 1))
            dve_heads(dve, moba, BB)
            cut_phase(dve, False, "in1", no_evict)
            phase_over(dve, "in1")
            dve.tensor_scalar(ablk[:, 48:52, :], ablk[:, 48:52, :], SCALE, None, ALU.mult).then_inc(q_scaled, 1)
            dve.wait_ge(silu_done, 4)
            dve.wait_ge(s_tmp, 24)
            for step in range(MH + 2):
                dve_heads(dve, heads_b, step, step + 1)
                if step < 4:
                    o = ablk[:, 24 + 3 * step:27 + 3 * step, :]
                    dve.tensor_tensor(o, o, ablk[:, 36 + 3 * step:39 + 3 * step, :], ALU.mult).then_inc(b_val, 1)
                if 1 <= step < 5:
                    q = step - 1
                    dve.wait_ge(b_hi, q + 1)
                    dve.tensor_tensor(al[:, 3 * q:3 * q + 3, :], ablk[:, 24 + 3 * q:27 + 3 * q, :],
                                      ah[:, 3 * q:3 * q + 3, :].bitcast(F32), ALU.subtract).then_inc(b_lo, 1)
            cut_phase(dve, False, "out1", residual_evict(dve, "out1", ALPHA, norm=4))
            dve_norm(dve, 4, split=False)
            for n in range(1, 8, 2):
                dve.wait_ge(o_t, n + 1)
                dve.wait_ge(o_sb, n)
                dve.tensor_copy(sflat[:, n * 512:(n + 1) * 512], G[:, n % 4, :]).then_inc(o_sb, 1)


_INS = {"x": "x", "norm1": "norm1_gain", "w_in": "w_in", "lbp": "hgrn_lb_param", "hgain": "hgrn_norm_gain",
        "fox_bias": "fox_gate_bias", "w_out": "w_out", "norm2": "norm2_gain", "w_ffn_gate": "w_ffn_gate",
        "w_ffn_up": "w_ffn_up", "conv_w": "ffn_conv_w", "conv_b": "ffn_conv_b", "w_ffn_down": "w_ffn_down",
        "final": "final_norm_gain", "mem": "mem_2", "w_in_2": "w_in_2", "w_out_2": "w_out_2",
        "w_mem_kv": "w_mem_kv_2", "ln_g": "ln_g_2", "ln_b": "ln_b_2", "pool_w": "pool_w_2",
        "pool_scale": "pool_scale_2", "w_kv": "w_kv_shared_2"}
_FIRST = ("x", "mem", "w_in", "w_out", "w_ffn_gate", "w_ffn_up", "conv_w", "w_ffn_down", "pool_w")


def kernel(**inputs):
    import numpy as np
    import concourse.bacc as bacc
    from concourse.bass_utils import run_bass_kernel_spmd

    nc = bacc.Bacc("TRN2", target_bir_lowering=False, num_devices=1)
    arrays, aps = {}, {}
    for key, name in _INS.items():
        a = np.ascontiguousarray(inputs[name])
        arrays[f"in_{name}"] = a
        ap = nc.dram_tensor(f"in_{name}", a.shape, mybir.dt.from_np(a.dtype), kind="ExternalInput").ap()
        aps[key] = ap[0] if key in _FIRST else ap.unsqueeze(0) if key == "final" else ap
    result = nc.dram_tensor("result", (1, TOK, D), F32, kind="ExternalOutput").ap()
    aps["result"] = result[0]
    program(nc, aps)
    r = run_bass_kernel_spmd(nc, [arrays], core_ids=[0])
    return r.results[0]["result"]
```
